# Optimizing a Trainium2 kernel written in Bass

```python
import math
import jax
import jax.numpy as jnp
from jax import lax
import numpy as np

D_MODEL = 1024
BATCH = 1
SEQ = 512
DEPTH = 2

GROUP_WIDTH = D_MODEL // 4
HEAD_DIM = 64
N_HEADS_A = GROUP_WIDTH // HEAD_DIM
DIFF_DH = HEAD_DIM // 2
N_HEADS_B = GROUP_WIDTH // HEAD_DIM
CONV_CH = GROUP_WIDTH
CONV_GROUPS = 4
CONV_K = 31
N_HEADS_D = GROUP_WIDTH // HEAD_DIM
DILATED_CFG = ((128, 1), (512, 4), (2048, 16))
GRID_W = 64
NA_KH_MAX = 8
NA_KW = 16
ROPE_THETA = 10000.0
Q_BLOCK = 128
N_GROUPS = 4
EXPERTS_PER_GROUP = 8
N_EXPERTS = N_GROUPS * EXPERTS_PER_GROUP
TOP_K_INNER = 2
D_EXPERT = D_MODEL // 2
MOE_BLOCK = 256
EPS = 1e-6
NEG_INF = -1e30

W_A = 3 * N_HEADS_A * HEAD_DIM
W_B = 3 * N_HEADS_B * HEAD_DIM
W_C = 2 * CONV_CH
W_D = 3 * N_HEADS_D * HEAD_DIM
P_IN = W_A + W_B + W_C + W_D

kernel_name = "hybrid_parallel_mixer_hmoe_block"

F32 = jnp.float32

def rms_norm(x, g):
    xf = x.astype(F32)
    y = xf * lax.rsqrt(jnp.mean(xf * xf, axis=-1, keepdims=True) + EPS)
    return (y * g.astype(F32)).astype(x.dtype)

def rotary(x):
    s, d = x.shape[1], x.shape[-1]
    inv = ROPE_THETA ** (-jnp.arange(0, d, 2, dtype=F32) / d)
    ang = jnp.arange(s, dtype=F32)[:, None] * inv[None, :]
    shp = (1, s) + (1,) * (x.ndim - 3) + (d // 2,)
    cos, sin = jnp.cos(ang).reshape(shp), jnp.sin(ang).reshape(shp)
    xf = x.astype(F32)
    x1, x2 = xf[..., : d // 2], xf[..., d // 2:]
    return jnp.concatenate([x1 * cos - x2 * sin, x2 * cos + x1 * sin], axis=-1).astype(x.dtype)

def diff_attention(q, k, v, lam_params, subln_g, layer_idx):
    b, s, h = q.shape[:3]
    lam_init = 0.8 - 0.6 * math.exp(-0.3 * layer_idx)
    lp = lam_params.astype(F32)
    lam = jnp.exp(jnp.sum(lp[0] * lp[1])) - jnp.exp(jnp.sum(lp[2] * lp[3])) + lam_init
    q, k = rotary(q), rotary(k)
    scale = DIFF_DH ** -0.5
    nqb = s // Q_BLOCK
    qb = jnp.moveaxis(q.reshape(b, nqb, Q_BLOCK, h, 2, DIFF_DH), 1, 0)

    def block(qi):
        sc = jnp.einsum('bqhce,bkhce->bhcqk', qi, k).astype(F32) * scale
        p = jax.nn.softmax(sc, axis=-1)
        a = p[:, :, 0] - lam * p[:, :, 1]
        return jnp.einsum('bhqk,bkhe->bqhe', a.astype(v.dtype), v)

    o = jnp.moveaxis(lax.map(block, qb), 0, 1).reshape(b, s, h, 2 * DIFF_DH)
    o = rms_norm(o, subln_g) * (1.0 - lam_init)
    return o.reshape(b, s, h * 2 * DIFF_DH)

def neighborhood_attention(q, k, v, rpb):
    b, s, h, e = q.shape
    rows = s // GRID_W
    kh = min(NA_KH_MAX, rows)
    kw = NA_KW
    qg = q.reshape(b, rows, GRID_W, h, e)
    kg = k.reshape(b, rows, GRID_W, h, e)
    vg = v.reshape(b, rows, GRID_W, h, e)
    ri = jnp.arange(rows)
    ci = jnp.arange(GRID_W)
    row_start = jnp.clip(ri - kh // 2, 0, rows - kh)
    row_idx = row_start[:, None] + jnp.arange(kh)[None, :]
    col_start = jnp.clip(ci - kw // 2, 0, GRID_W - kw)
    col_ok = (ci[None, :] >= col_start[:, None]) & (ci[None, :] < col_start[:, None] + kw)
    kr = kg[:, row_idx]
    vr = vg[:, row_idx]
    dr = row_idx - ri[:, None] + NA_KH_MAX - 1
    dc = jnp.clip(ci[None, :] - ci[:, None], -(kw - 1), kw - 1) + kw - 1
    bias = rpb.astype(F32)[:, dr[:, None, :, None], dc[None, :, None, :]]
    sc = jnp.einsum('bijhe,biawhe->bhijaw', qg, kr).astype(F32) * (e ** -0.5) + bias[None]
    sc = jnp.where(col_ok[:, None, :], sc, NEG_INF)
    p = jax.nn.softmax(sc.reshape(b, h, rows, GRID_W, kh * GRID_W), axis=-1).reshape(sc.shape)
    o = jnp.einsum('bhijaw,biawhe->bijhe', p.astype(v.dtype), vr)
    return o.reshape(b, s, h * e)

def conformer_conv(u, w_dw, b_dw, g_n, b_n):
    a, g = jnp.split(u, 2, axis=-1)
    z = a * jax.nn.sigmoid(g)
    z = lax.conv_general_dilated(
        z, w_dw[:, None, :].astype(z.dtype), window_strides=(1,),
        padding=[(CONV_K // 2, CONV_K // 2)], dimension_numbers=('NWC', 'WIO', 'NWC'),
        feature_group_count=CONV_CH) + b_dw.astype(z.dtype)
    b, s, ch = z.shape
    zf = z.astype(F32).reshape(b, s, CONV_GROUPS, ch // CONV_GROUPS)
    mu = jnp.mean(zf, axis=-1, keepdims=True)
    var = jnp.mean(jnp.square(zf - mu), axis=-1, keepdims=True)
    zn = ((zf - mu) * lax.rsqrt(var + EPS)).reshape(b, s, ch) * g_n.astype(F32) + b_n.astype(F32)
    return jax.nn.silu(zn).astype(u.dtype)

def dilated_branch(q, k, v, dilation, n_side):
    b, s, h, e = q.shape
    L = s // dilation
    blk = n_side
    nb = -(-L // blk)
    Lp = nb * blk

    def split(t):
        return t.reshape(b, L, dilation, h, e).transpose(0, 2, 1, 3, 4).reshape(b * dilation, L, h, e)

    qs, ks, vs = split(q), split(k), split(v)
    qb = jnp.pad(qs, ((0, 0), (0, Lp - L), (0, 0), (0, 0))).reshape(-1, nb, blk, h, e)

    def band(t):
        tp = jnp.pad(t, ((0, 0), (blk, Lp - L + blk), (0, 0), (0, 0))).reshape(-1, nb + 2, blk, h, e)
        return jnp.concatenate([tp[:, :-2], tp[:, 1:-1], tp[:, 2:]], axis=2)

    kb, vb = band(ks), band(vs)
    qpos = jnp.arange(nb)[:, None] * blk + jnp.arange(blk)[None, :]
    kpos = jnp.arange(nb)[:, None] * blk - blk + jnp.arange(3 * blk)[None, :]
    rel = kpos[:, None, :] - qpos[:, :, None]
    ok = (jnp.abs(rel) <= n_side) & (kpos[:, None, :] >= 0) & (kpos[:, None, :] < L)
    sc = jnp.einsum('ncqhe,nckhe->nhcqk', qb, kb).astype(F32) * (e ** -0.5)
    sc = jnp.where(ok, sc, NEG_INF)
    m = jnp.max(sc, axis=-1, keepdims=True)
    pe = jnp.exp(sc - m)
    l = jnp.sum(pe, axis=-1, keepdims=True)
    o = jnp.einsum('nhcqk,nckhe->ncqhe', (pe / l).astype(v.dtype), vb)
    lse = (m + jnp.log(l))[..., 0]

    def merge(t):
        t = t.reshape((b, dilation, Lp) + t.shape[2:])[:, :, :L]
        t = jnp.swapaxes(t, 1, 2)
        return t.reshape((b, s) + t.shape[3:])

    o = merge(o.reshape(b * dilation, Lp, h, e))
    lse = merge(jnp.transpose(lse, (0, 2, 3, 1)).reshape(b * dilation, Lp, h))
    return o, lse

def dilated_attention(q, k, v):
    b, s, h, e = q.shape
    q, k = rotary(q), rotary(k)
    outs, lses = [], []
    for window, dil in DILATED_CFG:
        o, lse = dilated_branch(q, k, v, dil, window // (2 * dil))
        outs.append(o)
        lses.append(lse)
    wts = jax.nn.softmax(jnp.stack(lses, axis=0), axis=0)
    o = jnp.einsum('gbsh,gbshe->bshe', wts, jnp.stack(outs, axis=0).astype(F32))
    return o.astype(v.dtype).reshape(b, s, h * e)

def expert_dispatch(xt, eid, gates, w_gate, w_up, w_down):
    T, d = xt.shape
    A = T * TOP_K_INNER
    flat_e = eid.reshape(-1)
    flat_tok = jnp.repeat(jnp.arange(T), TOP_K_INNER, total_repeat_length=A)
    flat_g = gates.reshape(-1)
    order = jnp.argsort(flat_e)
    se, stok, sg = flat_e[order], flat_tok[order], flat_g[order]
    counts = jnp.bincount(flat_e, length=N_EXPERTS)
    seg_start = jnp.cumsum(counts) - counts
    padded = (counts + MOE_BLOCK - 1) // MOE_BLOCK * MOE_BLOCK
    pad_end = jnp.cumsum(padded)
    pad_start = pad_end - padded
    dest = pad_start[se] + jnp.arange(A) - seg_start[se]
    nblk = A // MOE_BLOCK + N_EXPERTS
    buf_tok = jnp.zeros((nblk * MOE_BLOCK,), jnp.int32).at[dest].set(stok.astype(jnp.int32))
    blk_e = jnp.minimum(jnp.searchsorted(pad_end, jnp.arange(nblk) * MOE_BLOCK, side='right'), N_EXPERTS - 1)
    xb = xt[buf_tok].reshape(nblk, MOE_BLOCK, d)

    def run(args):
        xe, e_i = args
        hdn = jax.nn.silu(xe @ w_gate[e_i]) * (xe @ w_up[e_i])
        return hdn @ w_down[e_i]

    yb = lax.map(run, (xb, blk_e)).reshape(nblk * MOE_BLOCK, d)
    contrib = yb[dest].astype(F32) * sg[:, None]
    return jnp.zeros((T, d), F32).at[stok].add(contrib).astype(xt.dtype)

def hier_moe(h, w_rg, w_re, w_gate, w_up, w_down):
    b, s, d = h.shape
    xt = h.reshape(-1, d)
    lg = (xt @ w_rg).astype(F32)
    pg = jax.nn.softmax(lg, axis=-1)
    grp = jnp.argmax(lg, axis=-1)
    p_grp = jnp.take_along_axis(pg, grp[:, None], axis=-1)
    le = jnp.einsum('td,gde->tge', xt, w_re).astype(F32)
    le = jnp.take_along_axis(le, grp[:, None, None], axis=1)[:, 0]
    top_v, top_i = lax.top_k(le, TOP_K_INNER)
    gates = p_grp * jax.nn.softmax(top_v, axis=-1)
    eid = grp[:, None] * EXPERTS_PER_GROUP + top_i
    return expert_dispatch(xt, eid, gates, w_gate, w_up, w_down).reshape(b, s, d)

def setup_inputs(seed: int = 0) -> dict:
    key = jax.random.key(seed)
    ks = jax.random.split(key, 24)
    L, D = DEPTH, D_MODEL
    nrm = lambda k, shp, sc: jax.random.normal(k, shp, F32) * sc
    return {
        "x": nrm(ks[0], (BATCH, SEQ, D), 1.0),
        "c": nrm(ks[1], (BATCH, D), 1.0),
        "w_ada": nrm(ks[2], (L, D, 6 * D), 0.5 * D ** -0.5),
        "b_ada": nrm(ks[3], (L, 6 * D), 0.01),
        "g_norm1": 1.0 + nrm(ks[4], (L, D), 0.05),
        "g_norm2": 1.0 + nrm(ks[5], (L, D), 0.05),
        "w_in": nrm(ks[6], (L, D, P_IN), D ** -0.5),
        "diff_lambda": nrm(ks[7], (L, 4, DIFF_DH), 0.1),
        "diff_subln": 1.0 + nrm(ks[8], (L, 2 * DIFF_DH), 0.05),
        "na_rpb": nrm(ks[9], (L, N_HEADS_B, 2 * NA_KH_MAX - 1, 2 * NA_KW - 1), 0.05),
        "conv_dw": nrm(ks[10], (L, CONV_K, CONV_CH), CONV_K ** -0.5),
        "conv_b": nrm(ks[11], (L, CONV_CH), 0.01),
        "conv_norm_g": 1.0 + nrm(ks[12], (L, CONV_CH), 0.05),
        "conv_norm_b": nrm(ks[13], (L, CONV_CH), 0.01),
        "w_out": nrm(ks[14], (L, D, D), D ** -0.5),
        "w_router_group": nrm(ks[15], (L, D, N_GROUPS), D ** -0.5),
        "w_router_expert": nrm(ks[16], (L, N_GROUPS, D, EXPERTS_PER_GROUP), D ** -0.5),
        "w_exp_gate": nrm(ks[17], (L, N_EXPERTS, D, D_EXPERT), D ** -0.5),
        "w_exp_up": nrm(ks[18], (L, N_EXPERTS, D, D_EXPERT), D ** -0.5),
        "w_exp_down": nrm(ks[19], (L, N_EXPERTS, D_EXPERT, D), D_EXPERT ** -0.5),
        "g_final": 1.0 + nrm(ks[20], (D,), 0.05),
    }

def reference(x, c, w_ada, b_ada, g_norm1, g_norm2, w_in, diff_lambda, diff_subln, na_rpb,
              conv_dw, conv_b, conv_norm_g, conv_norm_b, w_out, w_router_group, w_router_expert,
              w_exp_gate, w_exp_up, w_exp_down, g_final):
    b, s, d = x.shape
    ca = jax.nn.silu(c)
    for l in range(DEPTH):
        mod = ca @ w_ada[l] + b_ada[l]
        sh1, sc1, gt1, sh2, sc2, gt2 = [m[:, None, :] for m in jnp.split(mod, 6, axis=-1)]
        h = rms_norm(x, g_norm1[l]) * (1.0 + sc1) + sh1
        proj = h @ w_in[l]
        pa, pb, pc, pd = jnp.split(proj, [W_A, W_A + W_B, W_A + W_B + W_C], axis=-1)
        qa, ka, va = jnp.split(pa, 3, axis=-1)
        ya = diff_attention(qa.reshape(b, s, N_HEADS_A, 2, DIFF_DH),
                            ka.reshape(b, s, N_HEADS_A, 2, DIFF_DH),
                            va.reshape(b, s, N_HEADS_A, HEAD_DIM),
                            diff_lambda[l], diff_subln[l], l)
        qb_, kb_, vb_ = [t.reshape(b, s, N_HEADS_B, HEAD_DIM) for t in jnp.split(pb, 3, axis=-1)]
        yb = neighborhood_attention(qb_, kb_, vb_, na_rpb[l])
        yc = conformer_conv(pc, conv_dw[l], conv_b[l], conv_norm_g[l], conv_norm_b[l])
        qd, kd, vd = [t.reshape(b, s, N_HEADS_D, HEAD_DIM) for t in jnp.split(pd, 3, axis=-1)]
        yd = dilated_attention(qd, kd, vd)
        mix = jnp.concatenate([ya, yb, yc, yd], axis=-1) @ w_out[l]
        x = x + gt1 * mix
        h2 = rms_norm(x, g_norm2[l]) * (1.0 + sc2) + sh2
        x = x + gt2 * hier_moe(h2, w_router_group[l], w_router_expert[l],
                               w_exp_gate[l], w_exp_up[l], w_exp_down[l])
    return rms_norm(x, g_final)


_drawn_inputs = setup_inputs


def setup_inputs(seed=0):
    import zlib

    import numpy as np

    out = dict(_drawn_inputs(seed))
    spreads = {}
    factors = {'b_ada': 3.309,
     'g_norm1': 3.564,
     'diff_lambda': 6.464,
     'diff_subln': 4.313,
     'na_rpb': 8.0,
     'conv_b': 8.0,
     'conv_norm_g': 5.059,
     'conv_norm_b': 24.344}
    for name, (base, spread) in spreads.items():
        noise = np.random.default_rng([zlib.crc32(name.encode()), seed]).standard_normal(out[name].shape)
        drawn = base * np.exp(spread * noise) if base else spread * noise
        out[name] = jnp.asarray(drawn.astype(out[name].dtype))
    for name, factor in factors.items():
        out[name] = (out[name] * factor).astype(out[name].dtype)
    return out
```

```python
from contextlib import ExitStack

import concourse.bass as bass
from concourse import mybir

ALU = mybir.AluOpType
ACT = mybir.ActivationFunctionType
AX_X = mybir.AxisListType.X
F32 = mybir.dt.float32
I32 = mybir.dt.int32
U32 = mybir.dt.uint32

P = 128
D, S, DEPTH = 1024, 512, 2
TT = S // P
KD = D // P
NMOD = 6
GW = D // 4
HD = 64
DIFF = HD // 2
NH = GW // HD
P_IN = 3 * GW * 3 + 2 * GW
TAPS = 31
HALO = TAPS // 2
GRID_W, GRID_H, NA_W = 64, S // 64, 16
RPB_H, RPB_W = 15, 31
NG, EPG = 4, 8
NE = NG * EPG
DE = D // 2
KE = DE // P
NLOG = NG + NE
EPS = 1e-6
NEG = -1e30
HALF = P // 2
CAP = P
NBLK = S // CAP
SLOTS = 6
UNITS_ADA = NMOD * D // 512
WIN_COLS = [(6 * GW, 512), (8 * GW, 512), (10 * GW, 256), (0, 512), (2 * GW, 256), (3 * GW, 512), (5 * GW, 256)]
NORM1_UNITS = 4
GROUPS = "DAB"
FIRST_F = {"A": 0, "B": 2, "C": 4, "D": 6}
NO_SLOT = 4096
SUBLN_INIT = [0.8 - 0.6 * 2.718281828459045 ** (-0.3 * i) for i in range(DEPTH)]
CONSTS = {"ident": 128, "before": 128, "groupmean": 128, "ones": 128, "iota": NE, "bit": NE, "first": NG,
          "cosA": TT * DIFF, "sinA": TT * DIFF, "cosD": TT * HD, "sinD": TT * HD, "colmask": GRID_W, "eps": 1}
C_AT, _n = {}, 0
for _k, _w in CONSTS.items():
    C_AT[_k] = _n
    _n += _w
NCONST = _n
TILES = [(g, hp, t, h) for g in GROUPS for hp in range(2) for t in range(TT) for h in range(2)]
NTILE = len(TILES)
NOUT = NTILE // 2
NSTEP = NTILE + 7
NPROB = 4
NA0 = NOUT // 3
SUBLN_STEP = 4 * NA0 + 4


def leaves(step):
    j = (step - 6) // 2
    if step >= 6 and step % 2 == 0 and not NA0 <= j < 2 * NA0 and j < NOUT:
        return [j]
    j = NA0 + (step - SUBLN_STEP - 3) // 2
    return [j] if step % 2 and NA0 <= j < 2 * NA0 else []


ADA_LATER = [[(l, u) for u in range(NORM1_UNITS, UNITS_ADA)] + [(l + 1, u) for u in range(NORM1_UNITS) if l + 1 < DEPTH]
             for l in range(DEPTH)]
ADA_DONE = [NORM1_UNITS + sum(map(len, ADA_LATER[:l])) for l in range(DEPTH + 1)]


def ada_at(l, step):
    n = (step - 1) // 4
    return n if step % 4 == 1 and n < len(ADA_LATER[l]) else None


def unit_order():
    order = [("ada", 0, u) for u in range(NORM1_UNITS)]
    for l in range(DEPTH):
        order += [("win", l, n) for n in range(len(WIN_COLS))]
        order += [("ada",) + item for item in ADA_LATER[l]]
        order += [("wout", l, n) for n in range(2)]
        order += [("exp", l, n) for n in range(3 * NE)]
    return order


ORDER = unit_order()
UNIT = {key: n for n, key in enumerate(ORDER)}

NMAP = NTILE + NTILE // 3


def view(t, offset, dims):
    return bass.AP(t.tensor if isinstance(t, bass.AP) else t, offset, dims)


def plan_banks():
    used, at = [0] * 8, {}
    turn = {"mm": 0, "tr": 0, "o": 0}
    rings = {"mm": [0, 1, 2], "tr": [3, 4], "o": [5, 6]}

    def take(key, where):
        if isinstance(where, str):
            b = rings[where][turn[where] % len(rings[where])]
            turn[where] += 1
        else:
            b = where
        assert key not in at
        at[key] = (b, used[b])
        used[b] += 1

    for u in range(NORM1_UNITS):
        take((0, "ada", u), "mm")
        take((0, "mod", u), 7)
    for l in range(DEPTH):
        for t in range(TT):
            for half in range(2):
                take((l, "xT1", t, half), "tr")
        for i in range(4):
            take((l, "conv_in", i), "mm")
        for g in GROUPS:
            for t in range(TT):
                take((l, "qk", g, t), "mm")
                take((l, "qkT", g, t), "tr")
            for t in range(TT):
                take((l, "v", g, t), "mm")
        for i, (g, hp, t, h) in enumerate(TILES):
            for c in range(2 if g == "A" else 1):
                take((l, "score", i, c), "mm")
            take((l, "probT", i), "tr")
            if h == 0:
                take((l, "o", i // 2), "o")
        for step in range(NSTEP):
            if ada_at(l, step - 1) is not None:
                m, u = ADA_LATER[l][ada_at(l, step - 1)]
                take((m, "mod", u), 7)
            for j in leaves(step):
                take((l, "oT", j), 7)
            if ada_at(l, step) is not None:
                m, u = ADA_LATER[l][ada_at(l, step)]
                take((m, "ada", u), 7)
        for f in range(2):
            take((l, "mean", f), "mm")
            take((l, "var", f), "mm")
        for t in range(TT):
            for n in range(2):
                take((l, "out", t, n), "mm")
        for t in range(TT):
            for half in range(2):
                take((l, "xT2", t, half), "tr")
        take((l, "logits"), 7)
        take((l, "rank"), 5)
        for b in range(7):
            at[(l, "exp", b)] = (b, used[b])
            used[b] += NE
    return at


def program(nc, a):
    bank_of = plan_banks()
    ctx = ExitStack()
    with ctx:
        def sb(name, shape, dt=F32):
            return ctx.enter_context(nc.sbuf_tensor(name, shape, dt))

        def sem(name):
            return ctx.enter_context(nc.semaphore(name))

        def dram(name, shape, dt=F32):
            return nc.dram_tensor(name, shape, dt, kind="Internal").ap()

        xn2_d = [dram(f"xn2_d{l}", (S, D)) for l in range(DEPTH)]
        yexp_d = [dram(f"yexp_d{l}", (2 * S, D)) for l in range(DEPTH)]
        list_d = [dram(f"list_d{l}", (P * P, 1), I32) for l in range(DEPTH)]

        ps = ctx.enter_context(nc.psum_tensor("ps", [P, 8, 512], F32))

        ring = sb("ring", [P, SLOTS, KD, 512])
        x = sb("x", [P, TT, D])
        gate = sb("gate", [P, 2, D])
        hT = sb("hT", [P, KD, S])
        yT = hT
        arena = sb("arena", [P, 9216])
        xs = arena[:, 0:TT * D].rearrange("p (t d) -> p t d", t=TT)
        qkT = {g: arena[:, 2048 * i:2048 * i + 2048].rearrange("p (f s) -> p f s", f=4) for i, g in enumerate(GROUPS)}
        v = {g: arena[:, 6144 + 1024 * i:7168 + 1024 * i].rearrange("p (t c) -> p t c", t=TT) for i, g in enumerate(GROUPS)}
        xg = [arena[:, D * j:D * j + D] for j in range(2)]
        xgT = [arena[:, 2048 + D * j:2048 + D * j + D].rearrange("p (k s) -> p k s", k=KD) for j in range(2)]
        yexp = [arena[:, 4096 + D * j:4096 + D * j + D] for j in range(2)]
        sil = [arena[:, 6144 + DE * j:6144 + DE * j + DE] for j in range(2)]
        hid = [arena[:, 7168 + DE * j:7168 + DE * j + DE] for j in range(2)]
        hidT = [arena[:, 8192 + DE * j:8192 + DE * j + DE].rearrange("p (c s) -> p c s", c=KE) for j in range(2)]
        ycomb = [arena[:, 2 * D * j:2 * D * j + 2 * D].rearrange("p (k d) -> p k d", k=2) for j in range(2)]
        yA = v["D"].rearrange("p t c -> p (t c)").rearrange("p (j c) -> p j c", c=P)
        masks = sb("masks", [P, 2, S])
        bias_t = [qkT[g].rearrange("p f s -> p (f s)") for g in "DA"]
        prob = [sb(f"prob{i}", [P, S]) for i in range(NPROB)]
        probT = [sb(f"probT{i}", [P, TT, P]) for i in range(2)]
        z = sb("z", [P, 2, S + 2 * HALO])
        tmp = sb("tmp", [P, 2, S])
        ytok = sb("ytok", [P, P])
        cst = sb("cst", [P, NCONST])
        C = {k: cst[:, C_AT[k]:C_AT[k] + w] for k, w in CONSTS.items()}
        ca = sb("ca", [P, KD])
        csil = sb("csil", [P, KD])
        ca_rep = sb("ca_rep", [P, KD, 32])
        modb = sb("modb", [P, DEPTH * NMOD, KD])
        gcol = sb("gcol", [P, 2, DEPTH, KD])
        modc = sb("modc", [P, 4, KD])
        lamrow = probT[0][:, 0, :]
        lam = sb("lam", [P, 2 * DIFF])
        neglam = sb("neglam", [P, 4])
        subg = sb("subg", [P, HD])
        convw = sb("convw", [P, 2, TAPS])
        convp = sb("convp", [P, 3, 2])
        ssum = sb("ssum", [P, TT])
        rstd = sb("rstd", [P, TT])
        coef = sb("coef", [P, 2])
        oss = sb("oss", [P, 2 * NA0])
        mx = sb("mx", [P, NMAP])
        negm = sb("negm", [P, NMAP])
        lsum = sb("lsum", [P, NMAP])
        rinv = sb("rinv", [P, NMAP])
        wr = sb("wr", [P, KD, NLOG])
        lg = z[:, 0, HALO:HALO + TT * NLOG].rearrange("p (t e) -> p t e", t=TT)
        lem = z[:, 1, HALO:HALO + TT * NE].rearrange("p (t e) -> p t e", t=TT)
        rt = z[:, 0, 200:280]
        top8 = z[:, 0, 300:332].rearrange("p (t n) -> p t n", t=TT)
        idx8 = sb("idx8", [P, TT, 8], U32)
        hot = prob[0][:, 0:2 * TT * NE].rearrange("p (k t e) -> p k t e", k=2, t=TT)
        hots = prob[1][:, 0:TT * NE].rearrange("p (t e) -> p t e", t=TT)
        rkc = prob[1][:, 256:256 + TT * NE + NE]
        rk = rkc[:, 0:TT * NE].rearrange("p (t e) -> p t e", t=TT)
        hotr = prob[2][:, 0:2 * TT * NE].rearrange("p (k t e) -> p k t e", k=2, t=TT)
        over = sb("over", [P, DEPTH], I32)
        wide = [sb(f"wide{l}", [1, 2], I32) for l in range(DEPTH)]
        widef = sb("widef", [1, NE + 2])
        gates = sb("gates", [P, 2, TT])
        pos = sb("pos", [P, 2 * TT], I32)
        vals = sb("vals", [P, 2 * TT], I32)
        lst = masks[:, 0, 0:P].bitcast(I32)
        gidx = masks[:, 0, P:2 * P].bitcast(I32)
        empty = masks[:, 1, 0:P].bitcast(I32)
        gcolumn = sb("gcolumn", [P, 1], I32)
        scolumn = sb("scolumn", [P, 1], I32)

        slot_in = [sem(f"slot_in{s}") for s in range(SLOTS)]
        filled = [sem(f"bank_filled{b}") for b in range(8)]
        drained = [sem(f"bank_drained{b}") for b in range(8)]
        consts_in, x_in, ids_in = sem("consts_in"), sem("x_in"), sem("ids_in")
        params_in = sem("params_in")
        table_in = sem("table_in")
        mask_in = [sem(f"mask_in{j}") for j in range(2)]
        silu_ready, ca_ready = sem("silu_ready"), sem("ca_ready")
        dve_chain, pool_chain = sem("dve_chain"), sem("pool_chain")
        ada_in = sem("ada_in")
        mod_ready = sem("mod_ready")
        sq_summed = sem("sq_summed")
        sq_ready = sem("sq_ready")
        oss_ready, oss_root = sem("oss_ready"), sem("oss_root")
        xs_ready = sem("xs_ready")
        halo_ready = sem("halo_ready")
        sig_ready = sem("sig_ready")
        rot_ready = sem("rot_ready")
        max_ready = sem("max_ready")
        exp_ready = sem("exp_ready")
        mix_ready = sem("mix_ready")
        pv_done = sem("pv_done")
        yA_ready = sem("yA_ready")
        bias_in, bias_ready = sem("bias_in"), sem("bias_ready")
        conv_done = [sem(f"conv_done{f}") for f in range(2)]
        stat_ready = sem("stat_ready")
        norm_ready = sem("norm_ready")
        conv_ready = sem("conv_ready")
        mixed = sem("mixed")
        xn_out = sem("xn_out")
        rin_ready, rexp_ready = sem("rin_ready"), sem("rexp_ready")
        hots_ready = sem("hots_ready")
        pos_ready = sem("pos_ready")
        list_init, listed, list_in = sem("list_init"), sem("listed"), sem("list_in")
        gidx_ready = sem("gidx_ready")
        xg_in = [sem(f"xg_in{j}") for j in range(2)]
        yrow_out = [sem(f"yrow_out{j}") for j in range(2)]
        ycomb_in = [sem(f"ycomb_in{j}") for j in range(2)]
        over_ready = sem("over_ready")
        over_w = [sem(f"over_weights{l}") for l in range(DEPTH)]
        over_xg = [sem(f"over_tokens{l}") for l in range(DEPTH)]
        over_pe = [sem(f"over_pe{l}") for l in range(DEPTH)]
        over_act = [sem(f"over_act{l}") for l in range(DEPTH)]
        over_dve = [sem(f"over_dve{l}") for l in range(DEPTH)]
        over_out = [sem(f"over_rows{l}") for l in range(DEPTH)]
        x_done = sem("x_done")
        rin_lam, rexp_lam = sem("lambda_in"), sem("lambda_exp")
        gfin_in = sem("gfin_in")
        fin_ready, out_done = sem("fin_ready"), sem("out_done")
        N_PARAMS, N_TABLES = 6, 9

        def bank(key):
            return ps[:, bank_of[key][0], :]

        def bank4(key):
            return bank(key).rearrange("p (a s) -> p a s", a=4)

        def fills(ins, key):
            ins.then_inc(filled[bank_of[key][0]], 1)

        def drains(ins, key):
            ins.then_inc(drained[bank_of[key][0]], 1)

        def await_filled(eng, key):
            eng.wait_ge(filled[bank_of[key][0]], bank_of[key][1] + 1)

        def await_drained(eng, key):
            eng.wait_ge(drained[bank_of[key][0]], bank_of[key][1] + 1)

        def await_free(eng, key):
            if bank_of[key][1]:
                eng.wait_ge(drained[bank_of[key][0]], bank_of[key][1])

        def slot(unit):
            return ring[:, unit % SLOTS, :, :]

        def await_unit(eng, unit):
            eng.wait_ge(slot_in[unit % SLOTS], 16 * (unit // SLOTS + 1))

        def last_use(unit):
            kind, l, u = ORDER[unit]
            if kind == "ada":
                return l, "ada", u
            if kind == "win":
                return (l, "conv_in", 3) if u == 0 else (l, "qk" if u % 2 else "v", GROUPS[(u - 1) // 2], TT - 1)
            return (l, "out", TT - 1, u) if kind == "wout" else None

        def wide_words(eng, l):
            eng.wait_ge(over_ready, l + 1)
            return [eng.value_load(wide[l][0:1, j:j + 1], min_val=0, max_val=2 ** HE - 1) for j in range(2)]

        def by_width(eng, words, it, j, body):
            with eng.If(((words[j] >> it) & 1) > 0):
                body(P)
            with eng.Else():
                body(HALF)

        def on_overflow(eng, l):
            eng.wait_ge(over_ready, l + 1)
            return eng.If(eng.value_load(over[0:1, l:l + 1], min_val=0, max_val=1) > 0)

        maps = [(i, c) for i, tile in enumerate(TILES) for c in range(2 if tile[0] == "A" else 1)]
        map_no = {m: n for n, m in enumerate(maps)}
        NQK = len(GROUPS) * TT

        def prob_of(n):
            return prob[n % NPROB]

        def await_prob(eng, l, n):
            n -= NPROB
            if n >= NQK:
                await_filled(eng, (l, "probT", maps[n - NQK][0]))
            elif n >= 0:
                await_filled(eng, (l, "qkT", GROUPS[n // TT], n % TT))

        def expert_bank(l, b):
            return bank_of[(l, "exp", b)][1]

        HE = NE // 2

        def route(dve, link, l):
            key = (l, "logits")
            await_filled(dve, key)
            drains(dve.tensor_copy(lg.rearrange("p t e -> p (t e)"), bank(key)[:, 0:TT * NLOG]), key)
            await_drained(dve, key)
            gl = lg[:, :, 0:NG]
            W = 2 * (S + 2 * HALO)

            def r3(first, n=NG):
                return rt[:, first:first + TT * n].rearrange("p (t n) -> p t n", t=TT)

            def spread(first, n):
                return view(z, 200 + first, [[W, P], [1, TT], [0, n]])

            diff, dv, gmax, pgrp = 0, 16, 20, 24
            eq, vmax, hotg, e01 = 28, 44, 48, 64
            link(dve.tensor_reduce(rt[:, gmax:gmax + TT], gl, AX_X, ALU.max))
            dve.tensor_tensor(r3(diff), gl, spread(gmax, NG), ALU.subtract).then_inc(rin_ready, 1)
            link(dve.tensor_tensor(r3(eq), gl, spread(gmax, NG), ALU.is_equal))
            link(dve.tensor_tensor(r3(eq), r3(eq), view(cst, C_AT["first"], [[NCONST, P], [0, TT], [1, NG]]), ALU.mult))
            link(dve.tensor_reduce(rt[:, vmax:vmax + TT], r3(eq), AX_X, ALU.max))
            link(dve.tensor_tensor(r3(hotg), r3(eq), spread(vmax, NG), ALU.is_equal))
            link(dve.tensor_scalar(rt[:, hotg:hotg + 16], rt[:, hotg:hotg + 16], -1.0, -NEG, ALU.add, ALU.mult))
            for t in range(TT):
                last = dve.tensor_tensor(lem[:, t, :].rearrange("p (g e) -> p g e", g=NG),
                                         lg[:, t, NG:].rearrange("p (g e) -> p g e", g=NG),
                                         view(z, 200 + hotg + NG * t, [[W, P], [1, NG], [0, EPG]]), ALU.add)
            link(last)
            for t in range(TT):
                last = dve.max(top8[:, t, :], lem[:, t, :])
            link(last)
            for t in range(TT):
                last = dve.max_index(idx8[:, t, :], top8[:, t, :], lem[:, t, :])
            link(last)
            dve.tensor_tensor(rt[:, dv:dv + TT], top8[:, :, 1], top8[:, :, 0], ALU.subtract).then_inc(rin_ready, 1)
            e2 = rt[:, e01:e01 + 2 * TT].rearrange("p (k t) -> p k t", k=2)
            link(dve.tensor_copy(e2, idx8[:, :, 0:2].rearrange("p t k -> p k t")))
            iota = view(cst, C_AT["iota"], [[NCONST, P], [0, TT], [1, NE]])
            for k in range(2):
                last = dve.tensor_tensor(hot[:, k], iota, spread(e01 + TT * k, NE), ALU.is_equal)
            link(last)
            dve.tensor_tensor(hots, hot[:, 0], hot[:, 1], ALU.add).then_inc(hots_ready, 1)
            dve.wait_ge(rexp_ready, 2 * (l + 1))
            link(dve.tensor_reduce(rt[:, pgrp:pgrp + TT], r3(diff), AX_X, ALU.add))
            link(dve.tensor_scalar(gates[:, 0, :], rt[:, dv:dv + TT], 1.0, None, ALU.add))
            link(dve.tensor_tensor(gates[:, 0, :], gates[:, 0, :], rt[:, pgrp:pgrp + TT], ALU.mult))
            link(dve.reciprocal(gates[:, 0, :], gates[:, 0, :]))
            link(dve.tensor_tensor(gates[:, 1, :], gates[:, 0, :], rt[:, dv:dv + TT], ALU.mult))
            key = (l, "rank")
            await_filled(dve, key)
            drains(dve.tensor_copy(rkc, bank(key)[:, 0:TT * NE + NE]), key)
            await_drained(dve, key)
            link(dve.tensor_scalar(widef[:, 0:NE], rkc[0:1, TT * NE:], HALF + 0.5, None, ALU.is_ge))
            link(dve.tensor_tensor(widef[:, 0:NE], widef[:, 0:NE], C["bit"][0:1, :], ALU.mult))
            link(dve.tensor_reduce(widef[:, NE:NE + 2], widef[:, 0:NE].rearrange("p (i j) -> p j i", j=2), AX_X, ALU.add))
            link(dve.tensor_copy(wide[l][:, :], widef[:, NE:NE + 2]))
            link(dve.tensor_reduce(rt[:, 8:9], rkc[:, TT * NE:], AX_X, ALU.max))
            dve.tensor_scalar(over[:, l:l + 1], rt[:, 8:9], CAP + 0.5, None, ALU.is_ge).then_inc(over_ready, 1)
            for k in range(2):
                last = dve.tensor_tensor(hotr[:, k], hot[:, k], rk, ALU.mult)
            link(last)
            rank, acc = rt[:, 0:8], rt[:, 72:80]
            link(dve.tensor_reduce(rank, hotr.rearrange("p k t e -> p (k t) e"), AX_X, ALU.add))
            link(dve.scalar_tensor_tensor(acc, rank, float(P), rt[:, e01:e01 + 8], ALU.mult, ALU.add))
            for b in range(1, NBLK):
                link(dve.tensor_scalar(rt[:, 8:16], rank, float(CAP * b), float(NE - P * CAP), ALU.is_ge, ALU.mult))
                link(dve.tensor_tensor(acc, acc, rt[:, 8:16], ALU.add))
            dve.tensor_copy(pos[:, :], acc).then_inc(pos_ready, 1)
            dve.wait_ge(list_in, 16 * (l + 1))
            link(dve.tensor_scalar(gidx, lst, S, -S, ALU.is_ge, ALU.mult))
            dve.tensor_tensor(gidx, lst, gidx, ALU.add).then_inc(gidx_ready, 1)

        def experts_dve(dve, l):
            def at(b, e):
                return e + expert_bank(l, b)

            def expert_tokens(e, j):
                dve.wait_ge(filled[4], at(4, e) + 1)
                if not isinstance(e, int) or e >= 2:
                    dve.wait_ge(filled[1], at(1, e) - 1)
                for q in range(4):
                    k = 4 + q
                    last = dve.tensor_scalar(xgT[j][:, k, :], ps[:, 4, P * q:P * q + P], modc[:, 3, k:k + 1],
                                             modc[:, 2, k:k + 1], ALU.mult, ALU.add)
                last.then_inc(drained[4], 1)

            def expert_hidden(e, it, j):
                def body(w):
                    dve.wait_ge(filled[1], at(1, e) + 1)
                    dve.wait_ge(drained[0], at(0, e) + 1)
                    if not isinstance(e, int) or e >= 2:
                        dve.wait_ge(filled[2], at(2, e) - 1)
                    dve.tensor_tensor(hid[j][0:w, :], ps[P - w:P, 1, :], sil[j][0:w, :], ALU.mult).then_inc(drained[1], 1)
                by_width(dve, words, it, j, body)

            def expert_rows(e, it, j):
                def body(w):
                    dve.wait_ge(filled[6], at(6, e) + 1)
                    if not isinstance(it, int) or it >= 1 or l:
                        dve.wait_ge(yrow_out[j], 16 * it + 16 * l * HE)
                    dve.tensor_copy(yexp[j][0:w, 512:D], ps[P - w:P, 6, :]).then_inc(drained[6], 1)
                by_width(dve, words, it, j, body)

            words = wide_words(dve, l)
            expert_tokens(0, 0)
            expert_hidden(0, 0, 0)
            expert_tokens(1, 1)
            expert_hidden(1, 0, 1)
            expert_rows(0, 0, 0)
            expert_tokens(2, 0)
            expert_hidden(2, 1, 0)
            expert_rows(1, 0, 1)
            expert_tokens(3, 1)
            with dve.Fori(1, HE - 1) as it:
                expert_hidden(2 * it + 1, it, 1)
                expert_rows(2 * it, it, 0)
                expert_tokens(2 * it + 2, 0)
                expert_hidden(2 * it + 2, it + 1, 0)
                expert_rows(2 * it + 1, it, 1)
                expert_tokens(2 * it + 3, 1)
            expert_hidden(NE - 1, HE - 1, 1)
            expert_rows(NE - 2, HE - 1, 0)
            expert_rows(NE - 1, HE - 1, 1)
            with on_overflow(dve, l):
                with dve.Fori(0, NE * (NBLK - 1)) as n:
                    dve.wait_ge(over_pe[l], 4 * n + 1)
                    for q in range(4):
                        k = 4 + q
                        last = dve.tensor_scalar(xgT[0][:, k, :], ps[:, 4, P * q:P * q + P], modc[:, 3, k:k + 1],
                                                 modc[:, 2, k:k + 1], ALU.mult, ALU.add)
                    last.then_inc(over_dve[l], 1)
                    dve.wait_ge(over_act[l], 4 * n + 2)
                    dve.tensor_tensor(hid[0], ps[:, 1, :], sil[0], ALU.mult).then_inc(over_dve[l], 1)
                    dve.wait_ge(over_pe[l], 4 * n + 4)
                    dve.tensor_copy(yexp[0][:, 512:D], ps[:, 6, :]).then_inc(over_dve[l], 1)

        block = ctx.enter_context(nc.Block())

        @block.sync
        def _(sp):
            def load(unit, dst, src):
                old = unit - SLOTS
                if old >= 0:
                    key = last_use(old)
                    if key:
                        await_filled(sp, key)
                    else:
                        _, lo, e3 = ORDER[old]
                        e, c = divmod(e3, 3)
                        b = (0, 1, 6)[c]
                        sp.wait_ge(filled[b], expert_bank(lo, b) + e + 1)
                sp.dma_start(dst, src).then_inc(slot_in[unit % SLOTS], 16)

            def load_ada(l, u):
                unit = UNIT["ada", l, u]
                load(unit, slot(unit), a["w_ada"][l].rearrange("(p k) n -> p k n", k=KD)[:, :, 512 * u:512 * u + 512])

            sp.dma_start(ca[:, :], a["c"].rearrange("b (p k) -> (b p) k", k=KD)).then_inc(consts_in, 16)
            sp.dma_start(cst[:, :], a["consts"]).then_inc(consts_in, 16)
            for u in range(NORM1_UNITS):
                load_ada(0, u)
            for l in range(DEPTH):
                for n, (c0, w) in enumerate(WIN_COLS):
                    unit = UNIT["win", l, n]
                    load(unit, slot(unit)[:, :, 0:w], a["w_in"][l].rearrange("(p k) n -> p k n", k=KD)[:, :, c0:c0 + w])
                for m, u in ADA_LATER[l]:
                    load_ada(m, u)
                for n in range(2):
                    unit = UNIT["wout", l, n]
                    load(unit, slot(unit), a["w_out"][l].rearrange("(k p) n -> p k n", p=P)[:, :, 512 * n:512 * n + 512])
                w3 = [a[name][l].rearrange("(i j) (p k) n -> i j p (k n)", j=2, p=P)
                      for name in ("w_exp_gate", "w_exp_up", "w_exp_down")]
                for j in range(2):
                    for c in range(3):
                        unit = UNIT["exp", l, 3 * j] + c
                        load(unit, slot(unit).rearrange("p k n -> p (k n)"), w3[c][0, j])
                with sp.Fori(1, HE) as it:
                    for j in range(2):
                        for c, b in enumerate((0, 1, 6)):
                            unit = UNIT["exp", l, 3 * j] + c
                            sp.wait_ge(filled[b], 2 * it + (expert_bank(l, b) + j - 1))
                            sp.dma_start(slot(unit).rearrange("p k n -> p (k n)"), w3[c][it, j])\
                                .then_inc(slot_in[unit % SLOTS], 16)
                with on_overflow(sp, l):
                    sp.wait_ge(filled[6], expert_bank(l, 6) + NE)
                    sp.wait_ge(filled[1], expert_bank(l, 1) + NE)
                    flat = [a[name][l].rearrange("e (p k) n -> e p (k n)", p=P) for name in ("w_exp_gate", "w_exp_up", "w_exp_down")]
                    with sp.Fori(0, NBLK - 1) as b, sp.Fori(0, NE) as e:
                        sp.wait_ge(over_xg[l], 16 * NE * b + 16 * e + 16)
                        for c in range(3):
                            sp.dma_start(ring[:, c, :, :].rearrange("p k n -> p (k n)"), flat[c][e]).then_inc(over_w[l], 16)
                    sp.wait_ge(over_pe[l], 4 * NE * (NBLK - 1))

        @block.gpsimd
        def _(pool):
            chain = [0]

            def link(ins):
                chain[0] += 1
                ins.then_inc(pool_chain, 1)
                pool.wait_ge(pool_chain, chain[0])

            last_token, last_row = pool.to_reg(S - 1), pool.to_reg(2 * S - 1)
            pool.dma_start(vals[:, :], a["token_ids"]).then_inc(ids_in, 16)
            pool.memset(z[:, :, 0:HALO], 0.0).then_inc(halo_ready, 1)
            pool.memset(z[:, :, HALO + S:], 0.0).then_inc(halo_ready, 1)
            link(pool.memset(empty, NO_SLOT))
            for l in range(DEPTH):
                pool.dma_start(list_d[l].rearrange("(p e) o -> p (e o)", p=P), empty).then_inc(list_init, 16)

            for l in range(DEPTH):
                if l:
                    pool.wait_ge(x_done, TT * l)
                for n in range(2):
                    row = (3 * n + 2) * D
                    pool.dma_start(gate[:, n, :], view(a["b_ada"], l * NMOD * D + row, [[0, P], [1, D]])).then_inc(params_in, 16)
                pool.dma_start(lamrow, view(a["diff_lambda"], l * 4 * DIFF, [[0, P], [1, 4 * DIFF]])).then_inc(params_in, 16)
                pool.dma_start(subg[:, :], view(a["diff_subln"], l * HD, [[0, P], [1, HD]])).then_inc(params_in, 16)
                for f in range(2):
                    pool.dma_start(convw[:, f, :], a["conv_dw"][l, P * f:P * f + P, :])\
                        .then_inc(params_in, 16)
                for n, name in enumerate(("conv_b", "conv_norm_g", "conv_norm_b")):
                    pool.dma_start(convp[:, n, :], view(a[name], l * GW, [[1, P], [P, 2]]), allow_slow_non_contiguous=True).then_inc(table_in, 16)
                pool.dma_start(wr[:, :, 0:NG], a["w_router_group"][l].rearrange("(p k) g -> p k g", k=KD)).then_inc(table_in, 16)
                for g in range(NG):
                    pool.dma_start(wr[:, :, NG + EPG * g:NG + EPG * g + EPG],
                                   a["w_router_expert"][l, g].rearrange("(p k) e -> p k e", k=KD)).then_inc(table_in, 16)
                pool.wait_ge(list_init, 16 * DEPTH)
                pool.dma_start(masks[:, :, :], a["dilation"][0:2 * P, :].rearrange("(t p) k -> p t k", p=P)).then_inc(table_in, 16)

                pool.wait_ge(params_in, 16 * N_PARAMS * (l + 1))
                pool.wait_ge(table_in, 16 * N_TABLES * (l + 1))
                await_drained(pool, (l, "conv_in", 3))
                await_filled(pool, (l, "v", "B", TT - 1))
                acc = yT[:, FIRST_F["C"] + 1, :]
                link(pool.tensor_scalar(acc, z[:, 1, 0:S], convw[:, 1, 0:1], convp[:, 0, 1:2], ALU.mult, ALU.add))
                for k in range(1, TAPS):
                    part = yT[:, FIRST_F["B"] + k % 2, :]
                    link(pool.tensor_scalar(part, z[:, 1, k:k + S], convw[:, 1, k:k + 1], None, ALU.mult))
                    ins = pool.tensor_tensor(acc, acc, part, ALU.add)
                    if k < TAPS - 1:
                        link(ins)
                ins.then_inc(conv_done[1], 1)

                rows_b = RPB_H - 1
                for hp in range(2):
                    last = (hp + 1) * NTILE // 3 - 1
                    await_drained(pool, (l, "score", last, hp))
                    for h in range(2):
                        for up in range(2):
                            n = rows_b * GRID_W
                            pool.dma_start(bias_t[hp][GRID_W * up:GRID_W * up + GRID_W, n * h:n * h + n],
                                           a["rpb"][l, 2 * hp + h, :, GRID_W * (1 - up):GRID_W * (1 - up) + n])\
                                .then_inc(bias_in, 16)
                    pool.wait_ge(bias_in, 128 * l + 64 * (hp + 1))
                    for h in range(2):
                        n = rows_b * GRID_W
                        tab = bias_t[hp][:, n * h:n * h + n].rearrange("p (r w) -> p r w", w=GRID_W)
                        cm = view(cst, C_AT["colmask"], [[NCONST, P], [0, rows_b], [1, GRID_W]])
                        link(pool.tensor_scalar(tab, tab, HD ** 0.5, None, ALU.mult))
                        pool.tensor_tensor(tab, tab, cm, ALU.add).then_inc(bias_ready, 1)

                for t in range(TT):
                    for n in range(2):
                        await_drained(pool, (l, "out", t, n))
                        xh = x[:, t, 512 * n:512 * n + 512]
                        pool.tensor_tensor(xh, xh, tmp[:, n, :], ALU.add).then_inc(mixed, 1)

                pool.wait_ge(ids_in, 16)
                pool.wait_ge(pos_ready, l + 1)
                for n in range(2 * TT):
                    pool.indirect_dma_start(list_d[l], bass.IndirectOffsetOnAxis(ap=pos[:, n:n + 1], axis=0),
                                            vals[:, n:n + 1], None).then_inc(listed, 16)
                pool.wait_ge(listed, 16 * 2 * TT * (l + 1))
                pool.dma_start(lst, list_d[l].rearrange("(p e) o -> p (e o)", p=P)).then_inc(list_in, 16)

                pool.wait_ge(xn_out, 16 * TT * (l + 1))
                await_filled(pool, (l, "xT2", TT - 1, 1))
                for j in range(2):
                    link(pool.memset(xg[j], 0.0))
                pool.wait_ge(gidx_ready, l + 1)

                words = wide_words(pool, l)

                def gather(e):
                    def body(w):
                        if e >= 2:
                            pool.wait_ge(filled[4], expert_bank(l, 4) + e - 1)
                        pool.indirect_dma_start(xg[e % 2][0:w, :], None, xn2_d[l],
                                                bass.IndirectOffsetOnAxis(ap=gidx[0:w, e:e + 1], axis=0),
                                                bounds_check=last_token, oob_is_err=False).then_inc(xg_in[e % 2], 16)
                    by_width(pool, words, e // 2, e % 2, body)

                def scatter(e):
                    def body(w):
                        pool.wait_ge(drained[5], expert_bank(l, 5) + e + 1)
                        pool.wait_ge(drained[6], expert_bank(l, 6) + e + 1)
                        pool.indirect_dma_start(yexp_d[l], bass.IndirectOffsetOnAxis(ap=lst[0:w, e:e + 1], axis=0),
                                                yexp[e % 2][0:w, :], None, bounds_check=last_row, oob_is_err=False)\
                            .then_inc(yrow_out[e % 2], 16)
                    by_width(pool, words, e // 2, e % 2, body)

                for e in range(2):
                    gather(e)
                for e in range(NE):
                    if e + 2 < NE:
                        gather(e + 2)
                    scatter(e)
                for j in range(2):
                    pool.wait_ge(yrow_out[j], 16 * HE * (l + 1))
                with on_overflow(pool, l):
                    with pool.Fori(0, NE * (NBLK - 1)) as n:
                        pool.tensor_copy(gcolumn[:, :], gidx[:, bass.ds(n + NE, 1)])
                        pool.drain()
                        pool.indirect_dma_start(xg[0], None, xn2_d[l], bass.IndirectOffsetOnAxis(ap=gcolumn[:, :], axis=0),
                                                bounds_check=last_token, oob_is_err=False).then_inc(over_xg[l], 16)
                        pool.wait_ge(over_act[l], 4 * n + 4)
                        pool.wait_ge(over_dve[l], 3 * n + 3)
                        pool.tensor_copy(scolumn[:, :], lst[:, bass.ds(n + NE, 1)])
                        pool.drain()
                        pool.indirect_dma_start(yexp_d[l], bass.IndirectOffsetOnAxis(ap=scolumn[:, :], axis=0),
                                                yexp[0], None, bounds_check=last_row, oob_is_err=False)\
                            .then_inc(over_out[l], 16)
                        pool.wait_ge(over_out[l], 16 * n + 16)
                yv = yexp_d[l].rearrange("(k t p) d -> t p k d", k=2, p=P)
                for t in range(TT):
                    if t >= 2:
                        pool.wait_ge(x_done, TT * l + t - 1)
                    pool.dma_start(ycomb[t % 2], yv[t]).then_inc(ycomb_in[t % 2], 16)
            pool.wait_ge(x_done, TT * DEPTH)
            pool.dma_start(gate[:, 0, :], view(a["g_final"], 0, [[0, P], [1, D]])).then_inc(gfin_in, 16)
            for t in range(TT):
                pool.wait_ge(fin_ready, t + 1)
                pool.dma_start(a["out"].rearrange("b (t p) d -> t p (b d)", p=P)[t], x[:, t, :]).then_inc(out_done, 16)
            pool.wait_ge(out_done, 16 * TT)

        @block.tensor
        def _(pe):
            ident = C["ident"]

            def product(out, lhs, rhs, n=KD):
                for k in range(n):
                    last = pe.matmul(out, lhs(k), rhs(k), start=(k == 0), stop=(k == n - 1))
                return last

            def transposed_x(l, which):
                for t in range(TT):
                    pe.wait_ge(xs_ready, TT * (2 * l + which - 1) + t + 1)
                    for half in range(2):
                        key = (l, f"xT{which}", t, half)
                        await_free(pe, key)
                        for q in range(4):
                            k = 4 * half + q
                            last = pe.transpose(bank4(key)[:, q, :], xs[:, t, k:D:KD], ident)
                        fills(last, key)

            def ada(l, u):
                key, unit = (l, "ada", u), UNIT["ada", l, u]
                await_unit(pe, unit)
                await_free(pe, key)
                for r in range(2):
                    for q in range(4):
                        k = 4 * r + q
                        last = pe.matmul(bank(key)[32 * q:32 * q + 32, :], ca_rep[:, k, :], slot(unit)[:, k, :],
                                         start=(r == 0), stop=(r == 1), tile_position=(0, 32 * q))
                fills(last, key)

            def mod(l, u, part):
                key = (l, "mod", u)
                await_drained(pe, (l, "ada", u))
                await_free(pe, key)
                if u // 2 % 3 == 2:
                    fills(pe.matmul(bank(key), C["ones"], tmp[:, part, :], start=True, stop=True), key)
                    return
                p0 = HALF * (u % 2)
                for k in range(KD):
                    last = pe.matmul(bank(key)[p0:p0 + HALF, k:k + 1], tmp[:, part, k:512:KD], C["ones"][:, 0:1],
                                     start=True, stop=True, tile_position=(0, p0))
                fills(last, key)

            pe.wait_ge(consts_in, 32)
            pe.wait_ge(ca_ready, 1)
            for u in range(NORM1_UNITS + 1):
                if u < NORM1_UNITS:
                    ada(0, u)
                if u:
                    mod(0, u - 1, (u - 1) % 2)
            for l in range(DEPTH):
                transposed_x(l, 1)
                await_drained(pe, (l, "xT1", TT - 1, 0))
                await_drained(pe, (l, "xT1", TT - 1, 1))

                unit = UNIT["win", l, 0]
                await_unit(pe, unit)
                for i in range(4):
                    key = (l, "conv_in", i)
                    await_free(pe, key)
                    c0 = GW * (1 - i % 2) + P * (i // 2)
                    fills(product(bank(key), lambda k: slot(unit)[:, k, c0:c0 + P], lambda k: hT[:, k, :]), key)

                def qk_turn(g, t):
                    key = (l, "qkT", g, t)
                    n = GROUPS.index(g) * TT + t
                    pe.wait_ge(rot_ready, NQK * l + n + 1)
                    await_free(pe, key)
                    for f in range(4):
                        last = pe.transpose(bank4(key)[:, f, :], prob_of(n)[:, P * f:P * f + P], ident)
                    fills(last, key)

                for gi_, g in enumerate(GROUPS):
                    unit = UNIT["win", l, 1 + 2 * gi_]
                    await_unit(pe, unit)
                    for t in range(TT):
                        key = (l, "qk", g, t)
                        await_free(pe, key)
                        fills(product(bank(key), lambda k: hT[:, k, P * t:P * t + P], lambda k: slot(unit)[:, k, :]), key)
                        if t >= 2:
                            qk_turn(g, t - 2)
                    unit += 1
                    await_unit(pe, unit)
                    for t in range(TT):
                        key = (l, "v", g, t)
                        await_free(pe, key)
                        fills(product(bank(key)[:, 0:GW], lambda k: hT[:, k, P * t:P * t + P], lambda k: slot(unit)[:, k, 0:GW]), key)
                        if t < 2:
                            qk_turn(g, t + 2)

                def scores(i):
                    g, hp, t, h = TILES[i]
                    if i % (NTILE // 3) == 0:
                        await_drained(pe, (l, "qkT", g, TT - 1))
                    for c in range(2 if g == "A" else 1):
                        key = (l, "score", i, c)
                        p0, n = HD * h + DIFF * c, DIFF if g == "A" else HD
                        await_free(pe, key)
                        fills(pe.matmul(bank(key), qkT[g][p0:p0 + n, hp, P * t:P * t + P], qkT[g][p0:p0 + n, 2 + hp, :],
                                        start=True, stop=True), key)

                def turn(i):
                    g = TILES[i][0]
                    if g == "A":
                        pe.wait_ge(mix_ready, NTILE // 3 * l + i - NTILE // 3 + 1)
                    else:
                        pe.wait_ge(exp_ready, 2 * NTILE // 3 * l + (i if g == "D" else i - NTILE // 3) + 1)
                    key = (l, "probT", i)
                    await_free(pe, key)
                    src = prob_of(NQK + map_no[(i, 0)])
                    for kt in range(TT):
                        last = pe.transpose(bank4(key)[:, kt, :], src[:, P * kt:P * kt + P], ident)
                    fills(last, key)

                def attend(i):
                    g, hp, t, h = TILES[i]
                    key = (l, "o", i // 2)
                    if h == 0:
                        await_free(pe, key)
                    await_drained(pe, (l, "probT", i))
                    if i % (NTILE // 3) == 0:
                        await_drained(pe, (l, "v", g, TT - 1))
                    c0 = HD * (2 * hp + h)
                    last = product(bank(key)[:, HD * h:HD * h + HD], lambda k: probT[i % 2][:, k, :],
                                   lambda k: v[g][:, k, c0:c0 + HD], n=TT)
                    if h:
                        fills(last, key)
                    else:
                        last.then_inc(pv_done, 1)

                def leave(j):
                    key = (l, "oT", j)
                    await_free(pe, key)
                    if NA0 <= j < 2 * NA0:
                        pe.wait_ge(yA_ready, l + 1)
                    else:
                        await_drained(pe, (l, "o", j))
                    src = yA[:, j - NA0, :] if NA0 <= j < 2 * NA0 else ytok[:, :]
                    fills(pe.transpose(bank(key)[:, 0:P], src, ident), key)

                for i in range(NSTEP):
                    if i < NTILE:
                        scores(i)
                    if 2 <= i < NTILE + 2:
                        turn(i - 2)
                    if 3 <= i < NTILE + 3:
                        attend(i - 3)
                    if ada_at(l, i - 1) is not None:
                        n = ada_at(l, i - 1)
                        mod(*ADA_LATER[l][n], n % 2)
                    for j in leaves(i):
                        leave(j)
                    if ada_at(l, i) is not None:
                        ada(*ADA_LATER[l][ada_at(l, i)])

                for f in range(2):
                    pe.wait_ge(conv_done[f], l + 1)
                    key = (l, "mean", f)
                    await_free(pe, key)
                    fills(pe.matmul(bank(key), C["groupmean"], yT[:, FIRST_F["C"] + f, :], start=True, stop=True), key)
                    pe.wait_ge(stat_ready, 2 * l + f + 1)
                    key = (l, "var", f)
                    await_free(pe, key)
                    fills(pe.matmul(bank(key), C["groupmean"], tmp[:, f, :], start=True, stop=True), key)

                await_drained(pe, (l, "oT", NOUT - 1))
                await_drained(pe, (l, "oT", 2 * NA0 - 1))
                pe.wait_ge(conv_ready, 2 * (l + 1))
                for t in range(TT):
                    for n in range(2):
                        unit = UNIT["wout", l, n]
                        if t == 0:
                            await_unit(pe, unit)
                        key = (l, "out", t, n)
                        await_free(pe, key)
                        fills(product(bank(key), lambda k: yT[:, k, P * t:P * t + P], lambda k: slot(unit)[:, k, :]), key)

                transposed_x(l, 2)
                await_drained(pe, (l, "xT2", TT - 1, 0))
                await_drained(pe, (l, "xT2", TT - 1, 1))
                key = (l, "logits")
                await_free(pe, key)
                pe.wait_ge(table_in, 16 * N_TABLES * (l + 1))
                for t in range(TT):
                    last = product(bank(key)[:, NLOG * t:NLOG * t + NLOG], lambda k: hT[:, k, P * t:P * t + P], lambda k: wr[:, k, :])
                fills(last, key)
                key = (l, "rank")
                pe.wait_ge(hots_ready, l + 1)
                await_free(pe, key)
                for t in range(TT):
                    for s in range(t + 1):
                        pe.matmul(bank(key)[:, NE * t:NE * t + NE], C["before"] if s == t else C["ones"], hots[:, s, :],
                                  start=(s == 0), stop=(s == t))
                for s in range(TT):
                    last = pe.matmul(bank(key)[:, NE * TT:NE * TT + NE], C["ones"], hots[:, s, :], start=(s == 0), stop=(s == TT - 1))
                fills(last, key)

                def bank_e(b):
                    return ps[:, b, :]

                def at(b, e):
                    return e + expert_bank(l, b)

                def await_bank_free(b, e):
                    pe.wait_ge(drained[b], at(b, e))

                def turn_tokens(e, it, j):
                    pe.wait_ge(xg_in[j], 16 * it + 16 * (l * HE + 1))
                    for half in range(2):
                        b = 3 + half
                        await_bank_free(b, e)
                        for q in range(4):
                            k = 4 * half + q
                            last = pe.transpose(bank_e(b).rearrange("p (a s) -> p a s", a=4)[:, q, :], xg[j][:, k:D:KD], ident)
                        last.then_inc(filled[b], 1)

                def await_slot(it, unit):
                    pe.wait_ge(slot_in[unit % SLOTS], 16 * it + 16 * (unit // SLOTS + 1))

                def pair(w, outs, lhs, rhs, n):
                    if w == P:
                        return [product(outs[c], lhs, lambda k: rhs(c, k), n=n) for c in range(2)]
                    for k in range(n):
                        last = [pe.matmul(outs[c][HALF * c:HALF * c + HALF, :], lhs(k)[:, 0:HALF], rhs(c, k),
                                          start=(k == 0), stop=(k == n - 1), tile_position=(0, HALF * c)) for c in range(2)]
                    return last

                def gate_up(e, it, j):
                    unit = UNIT["exp", l, 3 * j]

                    def body(w):
                        pe.wait_ge(drained[3], at(3, e) + 1)
                        pe.wait_ge(drained[4], at(4, e) + 1)
                        for c in range(2):
                            await_slot(it, unit + c)
                            await_bank_free(c, e)
                        ends = pair(w, [bank_e(0), bank_e(1)], lambda k: xgT[j][:, k, :],
                                    lambda c, k: slot(unit + c)[:, k, :], KD)
                        for c in range(2):
                            ends[c].then_inc(filled[c], 1)
                    by_width(pe, words, it, j, body)

                def turn_hidden(e, j):
                    pe.wait_ge(drained[1], at(1, e) + 1)
                    await_bank_free(2, e)
                    for c in range(KE):
                        last = pe.transpose(ps[:, 2, P * c:P * c + P], hid[j][:, c:DE:KE], ident)
                    last.then_inc(filled[2], 1)

                def down(e, it, j):
                    unit = UNIT["exp", l, 3 * j] + 2
                    wdn = slot(unit).rearrange("p k n -> p (k n)").rearrange("p (c n) -> p c n", c=KE)

                    def body(w):
                        pe.wait_ge(drained[2], at(2, e) + 1)
                        await_slot(it, unit)
                        for n in range(2):
                            await_bank_free(5 + n, e)
                        ends = pair(w, [bank_e(5), bank_e(6)], lambda k: hidT[j][:, k, :],
                                    lambda c, k: wdn[:, k, 512 * c:512 * c + 512], KE)
                        for c in range(2):
                            ends[c].then_inc(filled[5 + c], 1)
                    by_width(pe, words, it, j, body)

                words = wide_words(pe, l)
                turn_tokens(0, 0, 0)
                gate_up(0, 0, 0)
                turn_tokens(1, 0, 1)
                with pe.Fori(0, HE - 1) as it:
                    turn_hidden(2 * it, 0)
                    gate_up(2 * it + 1, it, 1)
                    down(2 * it, it, 0)
                    turn_tokens(2 * it + 2, it + 1, 0)
                    turn_hidden(2 * it + 1, 1)
                    gate_up(2 * it + 2, it + 1, 0)
                    down(2 * it + 1, it, 1)
                    turn_tokens(2 * it + 3, it + 1, 1)
                turn_hidden(NE - 2, 0)
                gate_up(NE - 1, HE - 1, 1)
                down(NE - 2, HE - 1, 0)
                turn_hidden(NE - 1, 1)
                down(NE - 1, HE - 1, 1)
                with on_overflow(pe, l):
                    with pe.Fori(0, NE * (NBLK - 1)) as n:
                        pe.wait_ge(over_xg[l], 16 * n + 16)
                        for k in range(KD):
                            last = pe.transpose(ps[:, 3 + k // 4, P * (k % 4):P * (k % 4) + P], xg[0][:, k:D:KD], ident)
                        last.then_inc(over_pe[l], 1)
                        pe.wait_ge(over_act[l], 4 * n + 1)
                        pe.wait_ge(over_dve[l], 3 * n + 1)
                        pe.wait_ge(over_w[l], 48 * n + 48)
                        for c in range(2):
                            last = product(bank_e(c), lambda k: xgT[0][:, k, :], lambda k: ring[:, c, k, :])
                        last.then_inc(over_pe[l], 1)
                        pe.wait_ge(over_dve[l], 3 * n + 2)
                        for c in range(KE):
                            last = pe.transpose(ps[:, 2, P * c:P * c + P], hid[0][:, c:DE:KE], ident)
                        last.then_inc(over_pe[l], 1)
                        pe.wait_ge(over_act[l], 4 * n + 3)
                        w = ring[:, 2, :, :].rearrange("p k n -> p (k n)").rearrange("p (c n) -> p c n", c=KE)
                        for h in range(2):
                            last = product(bank_e(5 + h), lambda c: hidT[0][:, c, :], lambda c: w[:, c, 512 * h:512 * h + 512], n=KE)
                        last.then_inc(over_pe[l], 1)

        @block.scalar
        def _(act):
            act.dma_start(x[:, :, :], a["x"].rearrange("b (t p) d -> p (b t) d", p=P)).then_inc(x_in, 16)
            act.dma_start(modb[:, :, :], a["b_ada"].rearrange("l (v p k) -> p (l v) k", v=NMOD, k=KD)).then_inc(ada_in, 16)
            for n, name in enumerate(("g_norm1", "g_norm2")):
                act.dma_start(gcol[:, n], a[name].rearrange("l (p k) -> p l k", k=KD)).then_inc(ada_in, 16)
            act.wait_ge(consts_in, 32)
            act.activation(csil[:, :], ca[:, :], ACT.Silu).then_inc(silu_ready, 1)
            act.wait_ge(x_in, 16)

            def root_mean_square(t, before):
                s = ssum[:, t:t + 1]
                act.activation(xs[:, t, :], x[:, t, :], ACT.Square, accum_out=s).then_inc(sq_summed, 1)
                act.wait_ge(sq_summed, before + 1)
                act.activation(s, s, ACT.Sqrt, scale=1.0 / D, bias=C["eps"]).then_inc(sq_ready, 1)

            def squares(l, which):
                for t in range(TT):
                    if which == 1 and l:
                        act.wait_ge(x_done, TT * l)
                    if which == 2:
                        act.wait_ge(mixed, 2 * (TT * l + t + 1))
                    root_mean_square(t, TT * (2 * l + which - 1) + t)

            def modulate(l, which):
                act.wait_ge(mod_ready, ADA_DONE[l + which - 1])
                for t in range(TT):
                    key = (l, f"xT{which}", t, 0)
                    await_filled(act, key)
                    for q in range(4):
                        last = act.activation(hT[:, q, P * t:P * t + P], bank4(key)[:, q, :], ACT.Identity,
                                              scale=modc[:, 2 * which - 1, q:q + 1], bias=modc[:, 2 * which - 2, q:q + 1])
                    drains(last, key)

            def ada_out(l, u, part):
                await_filled(act, (l, "ada", u))
                drains(act.activation(tmp[:, part, :], bank((l, "ada", u)), ACT.Copy, scale=1 / 32), (l, "ada", u))

            for l in range(DEPTH):
                squares(l, 1)
                if l == 0:
                    for u in range(NORM1_UNITS):
                        ada_out(0, u, u % 2)
                modulate(l, 1)
                for f in range(2):
                    key = (l, "conv_in", 2 * f)
                    await_filled(act, key)
                    drains(act.activation(tmp[:, f, :], bank(key), ACT.Sigmoid), key)
                act.wait_ge(rin_lam, l + 1)
                act.activation(neglam[:, 0:2], neglam[:, 0:2], ACT.Exp).then_inc(rexp_lam, 1)
                for gi_, g in enumerate(GROUPS):
                    def qk_out(t):
                        key = (l, "qkT", g, t)
                        await_filled(act, key)
                        drains(act.activation(qkT[g][:, :, P * t:P * t + P], bank4(key), ACT.Copy), key)
                    for t in range(2):
                        qk_out(t)
                    for t in range(TT):
                        key = (l, "v", g, t)
                        await_filled(act, key)
                        drains(act.activation(v[g][:, t, :], bank(key)[:, 0:GW], ACT.Copy), key)
                        if t < 2:
                            qk_out(t + 2)

                def expo(i):
                    g = TILES[i][0]
                    for c in range(2 if g == "A" else 1):
                        n = map_no[(i, c)]
                        act.wait_ge(max_ready, NMAP * l + n + 1)
                        dst = prob_of(NQK + n)
                        if g == "A":
                            await_prob(act, l, NQK + n)
                            key = (l, "score", i, c)
                            drains(act.activation(dst[:, :], bank(key), ACT.Exp, scale=DIFF ** -0.5,
                                                  bias=negm[:, n:n + 1], accum_out=lsum[:, n:n + 1]), key)
                        else:
                            act.activation(dst[:, :], dst[:, :], ACT.Exp, scale=HD ** -0.5, bias=negm[:, n:n + 1],
                                           accum_out=lsum[:, n:n + 1]).then_inc(exp_ready, 1)

                def prob_out(i):
                    key = (l, "probT", i)
                    await_filled(act, key)
                    if i >= 2:
                        if i % 2:
                            await_filled(act, (l, "o", i // 2 - 1))
                        else:
                            act.wait_ge(pv_done, NOUT * l + i // 2)
                    drains(act.activation(probT[i % 2][:, :, :], bank4(key), ACT.Copy), key)

                def o_out(j):
                    key = (l, "oT", j)
                    g, hp, t, _ = TILES[2 * j]
                    await_filled(act, key)
                    if j == 2 * NA0:
                        act.wait_ge(conv_done[1], l + 1)
                    drains(act.activation(yT[:, FIRST_F[g] + hp, P * t:P * t + P], bank(key)[:, 0:P], ACT.Copy), key)

                for i in range(NSTEP):
                    if i < NTILE:
                        expo(i)
                    if i % 2 == 0 and 2 <= i < NTILE // 3 - 2:
                        n = i // 2 + 1
                        t = TILES[2 * n][2]
                        await_drained(act, (l, "score", 2 * n - 3, 0))
                        act.dma_start(masks[:, n % 2, :], a["dilation"][P * t:P * t + P, :]).then_inc(mask_in[n % 2], 16)
                    if 2 <= i < NTILE + 2:
                        prob_out(i - 2)
                    for j in leaves(i):
                        o_out(j)
                    n = ada_at(l, i)
                    if n is not None:
                        m, u = ADA_LATER[l][n]
                        if n >= 2:
                            await_filled(act, (ADA_LATER[l][n - 2][0], "mod", ADA_LATER[l][n - 2][1]))
                        if i > SUBLN_STEP:
                            act.wait_ge(oss_ready, l + 1)
                        ada_out(m, u, n % 2)
                    if i == SUBLN_STEP:
                        act.wait_ge(oss_ready, l + 1)
                        act.activation(oss[:, :], oss[:, :], ACT.Sqrt, scale=1.0 / HD, bias=C["eps"]).then_inc(oss_root, 1)
                for f in range(2):
                    key = (l, "var", f)
                    await_filled(act, key)
                    drains(act.activation(tmp[:, f, :], bank(key), ACT.Sqrt, bias=C["eps"]), key)
                for f in range(2):
                    act.wait_ge(norm_ready, 2 * l + f + 1)
                    act.activation(yT[:, FIRST_F["C"] + f, :], z[:, f, HALO:HALO + S], ACT.Silu,
                                   scale=convp[:, 1, f:f + 1], bias=convp[:, 2, f:f + 1]).then_inc(conv_ready, 1)
                squares(l, 2)
                for t in range(TT):
                    act.wait_ge(xs_ready, TT * (2 * l + 1) + t + 1)
                    act.dma_start(xn2_d[l].rearrange("(t p) d -> t p d", p=P)[t], xs[:, t, :]).then_inc(xn_out, 16)
                modulate(l, 2)
                for n in range(2):
                    act.wait_ge(rin_ready, 2 * l + n + 1)
                    r = rt[:, 0:16] if n == 0 else rt[:, 16:20]
                    act.activation(r, r, ACT.Exp).then_inc(rexp_ready, 1)

                def at(b, e):
                    return e + expert_bank(l, b)

                def expert_tokens(e, j):
                    act.wait_ge(filled[3], at(3, e) + 1)
                    if not isinstance(e, int) or e >= 2:
                        act.wait_ge(filled[1], at(1, e) - 1)
                    for q in range(4):
                        last = act.activation(xgT[j][:, q, :], ps[:, 3, P * q:P * q + P], ACT.Identity,
                                              scale=modc[:, 3, q:q + 1], bias=modc[:, 2, q:q + 1])
                    last.then_inc(drained[3], 1)

                def expert_silu(e, j):
                    act.wait_ge(filled[0], at(0, e) + 1)
                    if not isinstance(e, int) or e >= 2:
                        act.wait_ge(drained[1], at(1, e) - 1)
                    act.activation(sil[j], ps[:, 0, :], ACT.Silu).then_inc(drained[0], 1)

                def expert_hidden(e, j):
                    act.wait_ge(filled[2], at(2, e) + 1)
                    if not isinstance(e, int) or e >= 2:
                        act.wait_ge(filled[6], at(6, e) - 1)
                    act.activation(hidT[j].rearrange("p c s -> p (c s)"), ps[:, 2, :], ACT.Copy).then_inc(drained[2], 1)

                def expert_rows(e, it, j):
                    def body(w):
                        act.wait_ge(filled[5], at(5, e) + 1)
                        if not isinstance(it, int) or it >= 1 or l:
                            act.wait_ge(yrow_out[j], 16 * it + 16 * l * HE)
                        act.activation(yexp[j][0:w, 0:512], ps[0:w, 5, :], ACT.Copy).then_inc(drained[5], 1)
                    by_width(act, words, it, j, body)

                words = wide_words(act, l)
                expert_tokens(0, 0)
                expert_silu(0, 0)
                expert_tokens(1, 1)
                expert_hidden(0, 0)
                expert_silu(1, 1)
                expert_rows(0, 0, 0)
                expert_tokens(2, 0)
                expert_hidden(1, 1)
                expert_silu(2, 0)
                expert_rows(1, 0, 1)
                expert_tokens(3, 1)
                with act.Fori(1, HE - 1) as it:
                    expert_hidden(2 * it, 0)
                    expert_silu(2 * it + 1, 1)
                    expert_rows(2 * it, it, 0)
                    expert_tokens(2 * it + 2, 0)
                    expert_hidden(2 * it + 1, 1)
                    expert_silu(2 * it + 2, 0)
                    expert_rows(2 * it + 1, it, 1)
                    expert_tokens(2 * it + 3, 1)
                expert_hidden(NE - 2, 0)
                expert_silu(NE - 1, 1)
                expert_rows(NE - 2, HE - 1, 0)
                expert_hidden(NE - 1, 1)
                expert_rows(NE - 1, HE - 1, 1)
                with on_overflow(act, l):
                    with act.Fori(0, NE * (NBLK - 1)) as n:
                        act.wait_ge(over_pe[l], 4 * n + 1)
                        for q in range(4):
                            last = act.activation(xgT[0][:, q, :], ps[:, 3, P * q:P * q + P], ACT.Identity,
                                                  scale=modc[:, 3, q:q + 1], bias=modc[:, 2, q:q + 1])
                        last.then_inc(over_act[l], 1)
                        act.wait_ge(over_pe[l], 4 * n + 2)
                        act.activation(sil[0], ps[:, 0, :], ACT.Silu).then_inc(over_act[l], 1)
                        act.wait_ge(over_pe[l], 4 * n + 3)
                        act.activation(hidT[0].rearrange("p c s -> p (c s)"), ps[:, 2, :], ACT.Copy).then_inc(over_act[l], 1)
                        act.wait_ge(over_pe[l], 4 * n + 4)
                        act.activation(yexp[0][:, 0:512], ps[:, 5, :], ACT.Copy).then_inc(over_act[l], 1)
            act.wait_ge(x_done, TT * DEPTH)
            for t in range(TT):
                root_mean_square(t, TT * 2 * DEPTH + t)

        @block.vector
        def _(dve):
            chain = [0]

            def link(ins):
                chain[0] += 1
                ins.then_inc(dve_chain, 1)
                dve.wait_ge(dve_chain, chain[0])

            dve.wait_ge(consts_in, 32)
            dve.wait_ge(silu_ready, 1)
            dve.tensor_tensor(ca_rep[:, :, :], view(cst, C_AT["ones"], [[NCONST, P], [0, KD], [1, 32]]),
                              view(csil, 0, [[KD, P], [1, KD], [0, 32]]), ALU.mult).then_inc(ca_ready, 1)

            def normalise(l, which):
                for t in range(TT):
                    dve.wait_ge(sq_ready, TT * (2 * l + which - 1) + t + 1)
                    r = rstd[:, t:t + 1]
                    link(dve.reciprocal(r, ssum[:, t:t + 1]))
                    dve.tensor_scalar(xs[:, t, :], x[:, t, :], r, None, ALU.mult).then_inc(xs_ready, 1)

            def modulate(l, which):
                for t in range(TT):
                    key = (l, f"xT{which}", t, 1)
                    await_filled(dve, key)
                    for q in range(4):
                        k = 4 + q
                        last = dve.tensor_scalar(hT[:, k, P * t:P * t + P], bank4(key)[:, q, :], modc[:, 2 * which - 1, k:k + 1],
                                                 modc[:, 2 * which - 2, k:k + 1], ALU.mult, ALU.add)
                    drains(last, key)

            def mod_out(l, u):
                key, m = (l, "mod", u), u // 2
                await_filled(dve, key)
                if m % 3 == 2:
                    gv = gate[:, m // 3, 512 * (u % 2):512 * (u % 2) + 512]
                    dve.tensor_tensor(gv, bank(key), gv, ALU.add).then_inc(dve_chain, 1)
                else:
                    p = slice(HALF * (u % 2), HALF * (u % 2) + HALF)
                    c = modc[p, 2 * (m // 3) + m % 3, :]
                    dve.tensor_tensor(c, bank(key)[p, 0:KD], modb[p, NMOD * l + m, :], ALU.add).then_inc(dve_chain, 1)
                chain[0] += 1
                dve.wait_ge(dve_chain, chain[0])
                if m % 3 == 1:
                    link(dve.scalar_tensor_tensor(c, c, 1.0, gcol[p, m // 3, l, :], ALU.add, ALU.mult))
                dve.sem_inc(mod_ready, 1)
                dve.sem_inc(drained[bank_of[key][0]], 1)

            dve.wait_ge(x_in, 16)
            dve.wait_ge(ada_in, 48)
            for l in range(DEPTH):
                normalise(l, 1)
                if l == 0:
                    for u in range(NORM1_UNITS):
                        mod_out(0, u)
                dve.wait_ge(mod_ready, ADA_DONE[l])
                modulate(l, 1)
                dve.wait_ge(params_in, 16 * N_PARAMS * (l + 1))
                lv = lamrow.rearrange("p (a b c) -> p a b c", a=2, b=2)
                link(dve.tensor_tensor(lam[:, :].rearrange("p (a c) -> p a c", a=2), lv[:, :, 0, :], lv[:, :, 1, :], ALU.mult))
                dve.tensor_reduce(neglam[:, 0:2], lam[:, :].rearrange("p (a c) -> p a c", a=2), AX_X, ALU.add).then_inc(rin_lam, 1)
                dve.wait_ge(rexp_lam, l + 1)
                link(dve.tensor_tensor(neglam[:, 2:3], neglam[:, 1:2], neglam[:, 0:1], ALU.subtract))
                link(dve.tensor_scalar(neglam[:, 2:3], neglam[:, 2:3], -SUBLN_INIT[l], None, ALU.add))
                link(dve.tensor_scalar(subg[:, :], subg[:, :], 1.0 - SUBLN_INIT[l], None, ALU.mult))
                dve.wait_ge(halo_ready, 2)
                for f in range(2):
                    key = (l, "conv_in", 2 * f + 1)
                    await_drained(dve, (l, "conv_in", 2 * f))
                    await_filled(dve, key)
                    drains(dve.tensor_tensor(z[:, f, HALO:HALO + S], bank(key), tmp[:, f, :], ALU.mult), key)
                for gi_, g in enumerate(GROUPS):
                    for t in range(TT):
                        key, n = (l, "qk", g, t), gi_ * TT + t
                        await_filled(dve, key)
                        await_prob(dve, l, n)
                        if n:
                            dve.wait_ge(rot_ready, NQK * l + n)
                        else:
                            await_drained(dve, (l, "conv_in", 3))
                        dst = prob_of(n)
                        if g == "B":
                            drains(dve.tensor_copy(dst[:, :], bank(key)), key)
                            dve.wait_ge(drained[bank_of[key][0]], bank_of[key][1] + 1)
                            dve.sem_inc(rot_ready, 1)
                            continue
                        w = HD if g == "D" else DIFF
                        hw, ng = w // 2, 512 // w
                        cos = view(cst, C_AT["cos" + g] + w * t, [[NCONST, P], [0, ng], [1, w]])
                        src = bank(key).rearrange("p (g w) -> p g w", w=w)
                        tc = tmp[:, 0, :].rearrange("p (g w) -> p g w", w=w)
                        tsn = tmp[:, 1, :].rearrange("p (g w) -> p g w", w=w)
                        dve.tensor_tensor(tc, src, cos, ALU.mult)
                        for half in range(2):
                            sin = view(cst, C_AT["sin" + g] + w * t + hw * half, [[NCONST, P], [0, ng], [1, hw]])
                            last = dve.tensor_tensor(tsn[:, :, hw * half:hw * half + hw], src[:, :, hw * (1 - half):hw * (2 - half)],
                                                     sin, ALU.mult)
                        drains(last, key)
                        await_drained(dve, key)
                        dve.tensor_tensor(dst[:, :], tmp[:, 0, :], tmp[:, 1, :], ALU.add).then_inc(rot_ready, 1)

                def maxima(i):
                    g, hp, t, h = TILES[i]
                    for c in range(2 if g == "A" else 1):
                        n = map_no[(i, c)]
                        key = (l, "score", i, c)
                        await_filled(dve, key)
                        if g == "A":
                            link(dve.tensor_reduce(mx[:, n:n + 1], bank(key), AX_X, ALU.max))
                            dve.tensor_scalar(negm[:, n:n + 1], mx[:, n:n + 1], -DIFF ** -0.5, None, ALU.mult).then_inc(max_ready, 1)
                            continue
                        if i == 0:
                            dve.wait_ge(table_in, 16 * N_TABLES * (l + 1))
                        if g == "B":
                            dve.wait_ge(bias_ready, 4 * l + 2 * (hp + 1))
                        if g == "D":
                            if i >= 4:
                                dve.wait_ge(mask_in[i // 2 % 2], 16 * (3 * l + (i // 2 - 2) // 2 + 1))
                            table = masks[:, i // 2 % 2, :]
                        else:
                            first = (RPB_H - 1) * GRID_W * h + (GRID_H - 2 - 2 * t) * GRID_W
                            table = bias_t[hp][:, first:first + S]
                        await_prob(dve, l, NQK + n)
                        drains(dve.tensor_tensor_reduce(prob_of(NQK + n)[:, :], bank(key), table, 1.0, -3.0e38, ALU.add, ALU.max,
                                                        mx[:, n:n + 1]), key)
                        await_drained(dve, key)
                        dve.tensor_scalar(negm[:, n:n + 1], mx[:, n:n + 1], -HD ** -0.5, None, ALU.mult).then_inc(max_ready, 1)

                def mix(i):
                    n = map_no[(i, 0)]
                    for c in range(2):
                        await_drained(dve, (l, "score", i, c))
                    link(dve.reciprocal(rinv[:, n:n + 2], lsum[:, n:n + 2]))
                    link(dve.tensor_tensor(coef[:, 0:1], lsum[:, n:n + 1], rinv[:, n + 1:n + 2], ALU.mult))
                    link(dve.tensor_tensor(coef[:, 1:2], coef[:, 0:1], neglam[:, 2:3], ALU.mult))
                    p0, p1 = prob_of(NQK + n), prob_of(NQK + n + 1)
                    dve.scalar_tensor_tensor(p0[:, :], p1[:, :], coef[:, 1:2], p0[:, :], ALU.mult, ALU.add).then_inc(mix_ready, 1)

                def heads_out(j):
                    g = TILES[2 * j][0]
                    key = (l, "o", j)
                    n = map_no[(2 * j, 0)]
                    step = 2 if g == "A" else 1
                    rv = view(rinv, n, [[NMAP, P], [step, 2], [0, HD]])
                    o = bank(key)[:, 0:P].rearrange("p (h e) -> p h e", h=2)
                    y = (yA[:, j - NA0, :] if g == "A" else ytok[:, :]).rearrange("p (h e) -> p h e", h=2)
                    if g != "A":
                        dve.wait_ge(exp_ready, 2 * NTILE // 3 * l + (2 * j if g == "D" else 2 * j - NTILE // 3) + 2)
                        link(dve.reciprocal(rinv[:, n:n + 2], lsum[:, n:n + 2]))
                    await_filled(dve, key)
                    if g != "A" and j:
                        await_filled(dve, (l, "oT", j - 1 if j != 2 * NA0 else NA0 - 1))
                    drains(dve.tensor_tensor(y, o, rv, ALU.mult), key)

                def subln(part):
                    y = yA.rearrange("p j (h e) -> p (j h) e", h=2)
                    if part == 0:
                        sq = tmp[:, :, :].rearrange("p a (j e) -> p (a j) e", e=HD)
                        await_drained(dve, (l, "o", 2 * NA0 - 1))
                        m, u = [ADA_LATER[l][n] for n in (ada_at(l, k) for k in range(SUBLN_STEP)) if n is not None][-1]
                        await_filled(dve, (m, "mod", u))
                        link(dve.tensor_tensor(sq, y, y, ALU.mult))
                        dve.tensor_reduce(oss[:, :], sq, AX_X, ALU.add).then_inc(oss_ready, 1)
                        return
                    dve.wait_ge(oss_root, l + 1)
                    link(dve.reciprocal(oss[:, :], oss[:, :]))
                    link(dve.tensor_tensor(y, y, view(oss, 0, [[2 * NA0, P], [1, 2 * NA0], [0, HD]]), ALU.mult))
                    dve.tensor_tensor(y, y, view(subg, 0, [[HD, P], [0, 2 * NA0], [1, HD]]), ALU.mult).then_inc(yA_ready, 1)

                def tap(k):
                    acc = yT[:, FIRST_F["C"], :]
                    if k == 0:
                        await_filled(dve, (l, "v", "B", TT - 1))
                        link(dve.tensor_scalar(acc, z[:, 0, 0:S], convw[:, 0, 0:1], convp[:, 0, 0:1], ALU.mult, ALU.add))
                    elif k < TAPS - 1:
                        link(dve.scalar_tensor_tensor(acc, z[:, 0, k:k + S], convw[:, 0, k:k + 1], acc, ALU.mult, ALU.add))
                    elif k == TAPS - 1:
                        dve.scalar_tensor_tensor(acc, z[:, 0, k:k + S], convw[:, 0, k:k + 1], acc, ALU.mult, ALU.add)\
                            .then_inc(conv_done[0], 1)

                for i in range(NTILE + 4):
                    if i < NTILE:
                        maxima(i)
                    if 1 <= i <= NTILE and TILES[i - 1][0] == "A":
                        mix(i - 1)
                    tap(i - 2) if i >= 2 else None
                    if i >= 5 and i % 2 == 1:
                        heads_out((i - 5) // 2)
                    if ada_at(l, i - 1) is not None:
                        mod_out(*ADA_LATER[l][ada_at(l, i - 1)])
                    if SUBLN_STEP <= i < SUBLN_STEP + 2:
                        subln(i - SUBLN_STEP)

                for f in range(2):
                    key = (l, "mean", f)
                    await_filled(dve, key)
                    zc = z[:, f, HALO:HALO + S]
                    drains(dve.tensor_tensor(zc, yT[:, FIRST_F["C"] + f, :], bank(key), ALU.subtract), key)
                    await_drained(dve, key)
                    dve.tensor_tensor(tmp[:, f, :], zc, zc, ALU.mult).then_inc(stat_ready, 1)
                    key = (l, "var", f)
                    await_filled(dve, key)
                    await_drained(dve, key)
                    link(dve.reciprocal(tmp[:, f, :], tmp[:, f, :]))
                    dve.tensor_tensor(zc, zc, tmp[:, f, :], ALU.mult).then_inc(norm_ready, 1)

                for t in range(TT):
                    for n in range(2):
                        key = (l, "out", t, n)
                        await_filled(dve, key)
                        if t:
                            dve.wait_ge(mixed, 2 * (TT * l + t - 1) + n + 1)
                        drains(dve.tensor_tensor(tmp[:, n, :], bank(key), gate[:, 0, 512 * n:512 * n + 512], ALU.mult), key)
                normalise(l, 2)
                modulate(l, 2)
                route(dve, link, l)
                experts_dve(dve, l)
                for t in range(TT):
                    dve.wait_ge(ycomb_in[t % 2], 16 * (2 * l + t // 2 + 1))
                    y0, y1 = ycomb[t % 2][:, 0, :], ycomb[t % 2][:, 1, :]
                    link(dve.tensor_scalar(y0, y0, gates[:, 0, t:t + 1], None, ALU.mult))
                    link(dve.scalar_tensor_tensor(y0, y1, gates[:, 1, t:t + 1], y0, ALU.mult, ALU.add))
                    link(dve.tensor_tensor(y0, y0, gate[:, 1, :], ALU.mult))
                    dve.tensor_tensor(x[:, t, :], x[:, t, :], y0, ALU.add).then_inc(x_done, 1)
                dve.wait_ge(x_done, TT * (l + 1))
            for t in range(TT):
                dve.wait_ge(sq_ready, TT * 2 * DEPTH + t + 1)
                r = rstd[:, t:t + 1]
                link(dve.reciprocal(r, ssum[:, t:t + 1]))
                link(dve.tensor_scalar(x[:, t, :], x[:, t, :], r, None, ALU.mult))
                if t == 0:
                    dve.wait_ge(gfin_in, 16)
                dve.tensor_tensor(x[:, t, :], x[:, t, :], gate[:, 0, :], ALU.mult).then_inc(fin_ready, 1)


_INS = ["x", "c", "na_rpb", "w_ada", "b_ada", "g_norm1", "g_norm2", "w_in", "diff_lambda", "diff_subln", "conv_dw", "conv_b",
        "conv_norm_g", "conv_norm_b", "w_out", "w_router_group", "w_router_expert", "w_exp_gate", "w_exp_up",
        "w_exp_down", "g_final"]


def shape_constants():
    import numpy as np
    out = {}
    out["ident"] = np.eye(P)
    out["before"] = np.triu(np.ones((P, P)), 1)
    out["groupmean"] = np.kron(np.eye(2), np.ones((HD, HD)) / HD)
    out["ones"] = np.ones((P, P))
    out["iota"] = np.tile(np.arange(NE), (P, 1))
    out["bit"] = np.tile(2.0 ** (np.arange(NE) // 2), (P, 1))
    out["first"] = np.tile(np.arange(NG, 0, -1), (P, 1))
    for g, w in (("A", DIFF), ("D", HD)):
        inv = np.float32(10000.0) ** (-np.arange(0, w, 2, dtype=np.float32) / np.float32(w))
        ang = (np.arange(S, dtype=np.float32)[:, None] * inv.astype(np.float32)[None, :]).astype(np.float64)
        cos, sin = np.cos(ang), np.sin(ang)
        for name, tab in (("cos", np.concatenate([cos, cos], 1)), ("sin", np.concatenate([-sin, sin], 1))):
            out[name + g] = tab.reshape(TT, P, w).transpose(1, 0, 2).reshape(P, TT * w)
    col = np.arange(GRID_W)
    start = np.clip(col - NA_W // 2, 0, GRID_W - NA_W)
    ok = (col[None] >= start[:, None]) & (col[None] < start[:, None] + NA_W)
    out["colmask"] = np.tile(np.where(ok, 0.0, NEG), (2, 1))
    out["eps"] = np.full((P, 1), EPS)
    table = np.concatenate([out[k] for k in CONSTS], 1).astype(np.float32)
    rel = np.arange(S)[None] - np.arange(S)[:, None]
    count = sum(((rel % dil == 0) & (np.abs(rel) <= win // (2 * dil) * dil)).astype(int)
                for win, dil in ((128, 1), (512, 4), (2048, 16)))
    dil = np.where(count > 0, HD ** 0.5 * np.log(np.maximum(count, 1)), NEG).astype(np.float32)
    ids = (np.arange(2 * TT)[None] * P + np.arange(P)[:, None]).astype(np.int32)
    return table, dil, ids


def kernel(**inputs):
    import numpy as np
    import concourse.bacc as bacc
    from concourse.bass_utils import run_bass_kernel_spmd

    nc = bacc.Bacc("TRN2", target_bir_lowering=False, num_devices=1)
    arrays = {n: np.ascontiguousarray(inputs[n]) for n in _INS}
    arrays["conv_dw"] = np.ascontiguousarray(np.transpose(arrays["conv_dw"], (0, 2, 1)))
    col = np.arange(GRID_W)
    dc = np.clip(col[None] - col[:, None], -(RPB_W // 2), RPB_W // 2) + RPB_W // 2
    arrays["rpb"] = np.ascontiguousarray(np.moveaxis(arrays.pop("na_rpb")[..., dc], 2, 3)).reshape(DEPTH, NH, GRID_W, RPB_H * GRID_W)
    arrays["consts"], arrays["dilation"], arrays["token_ids"] = shape_constants()
    aps = {n: nc.dram_tensor(f"in_{n}", v.shape, mybir.dt.from_np(v.dtype), kind="ExternalInput").ap()
           for n, v in arrays.items()}
    aps["out"] = nc.dram_tensor("out_0", (1, S, D), F32, kind="ExternalOutput").ap()
    program(nc, aps)
    r = run_bass_kernel_spmd(nc, [{f"in_{n}": v for n, v in arrays.items()}], core_ids=[0])
    return r.results[0]["out_0"]
```

```python
from contextlib import ExitStack

import concourse.bass as bass
from concourse import mybir

ALU = mybir.AluOpType
ACT = mybir.ActivationFunctionType
AX_X = mybir.AxisListType.X
F32 = mybir.dt.float32
I32 = mybir.dt.int32
U32 = mybir.dt.uint32

P = 128
D, S, DEPTH = 1024, 512, 2
TT = S // P
KD = D // P
NMOD = 6
GW = D // 4
HD = 64
DIFF = HD // 2
NH = GW // HD
P_IN = 3 * GW * 3 + 2 * GW
TAPS = 31
HALO = TAPS // 2
DVE_TAPS = 8
GRID_W, GRID_H, NA_W = 64, S // 64, 16
RPB_H, RPB_W = 15, 31
NG, EPG = 4, 8
NE = NG * EPG
DE = D // 2
KE = DE // P
NLOG = NG + NE
EPS = 1e-6
NEG = -1e30
HALF = P // 2
CAP = P
NBLK = S // CAP
SLOTS = 6
UNITS_ADA = NMOD * D // 512
WIN_COLS = [(6 * GW, 512), (8 * GW, 512), (10 * GW, 256), (0, 512), (2 * GW, 256), (3 * GW, 512), (5 * GW, 256)]
ADA_STEP = 4
NORM1_UNITS = 4
GROUPS = "DAB"
FIRST_F = {"A": 0, "B": 2, "C": 4, "D": 6}
NO_SLOT = 4096
SUBLN_INIT = [0.8 - 0.6 * 2.718281828459045 ** (-0.3 * i) for i in range(DEPTH)]
CONSTS = {"ident": 128, "before": 128, "groupmean": 128, "ones": 128, "iota": P, "ids": 2 * TT, "bit": NE, "first": NG,
          "cosA": TT * DIFF, "sinA": TT * DIFF, "cosD": TT * HD, "sinD": TT * HD, "colmask": GRID_W, "eps": 1}
C_AT, _n = {}, 0
for _k, _w in CONSTS.items():
    C_AT[_k] = _n
    _n += _w
NCONST = _n
TILES = [(g, hp, t, h) for g in GROUPS for hp in range(2) for t in range(TT) for h in range(2)]
NTILE = len(TILES)
NOUT = NTILE // 2
NSTEP = NTILE + 7
NPROB = 4
NA0 = NOUT // 3
SUBLN_STEP = 4 * NA0 + 4
ROOT_STEP = SUBLN_STEP + 1


def leaves(step):
    j = (step - 6) // 2
    if step >= 6 and step % 2 == 0 and not NA0 <= j < 2 * NA0 and j < NOUT:
        return [j]
    j = NA0 + (step - ROOT_STEP - 2) // 2
    return [j] if step % 2 and NA0 <= j < 2 * NA0 else []


ADA_LATER = [[(l, u) for u in range(NORM1_UNITS, UNITS_ADA)] for l in range(DEPTH)]
ADA_NEXT = [[(l + 1, u) for u in range(NORM1_UNITS) if l + 1 < DEPTH] for l in range(DEPTH)]


def ada_at(l, step):
    n = (step - 1) // ADA_STEP
    return n if step % ADA_STEP == 1 and n < len(ADA_LATER[l]) else None


def unit_order():
    order = [("ada", 0, u) for u in range(NORM1_UNITS)]
    for l in range(DEPTH):
        order += [("win", l, n) for n in range(len(WIN_COLS))]
        order += [("ada",) + item for item in ADA_LATER[l]]
        order += [("wout", l, n) for n in range(2)]
        order += [("ada",) + item for item in ADA_NEXT[l]]
        order += [("exp", l, n) for n in range(3 * NE)]
    return order


ORDER = unit_order()
UNIT = {key: n for n, key in enumerate(ORDER)}

NMAP = NTILE + NTILE // 3


def view(t, offset, dims):
    return bass.AP(t.tensor if isinstance(t, bass.AP) else t, offset, dims)


def plan_banks():
    used, at = [0] * 8, {}
    turn = {"mm": 0, "tr": 0, "o": 0, "xT": 0}
    rings = {"mm": [0, 1, 2], "tr": [3, 4], "o": [5, 6], "xT": [3, 4, 5, 6]}

    def take(key, where):
        if isinstance(where, str):
            b = rings[where][turn[where] % len(rings[where])]
            turn[where] += 1
        else:
            b = where
        assert key not in at
        at[key] = (b, used[b])
        used[b] += 1

    for u in range(NORM1_UNITS):
        take((0, "ada", u), "mm")
        take((0, "mod", u), 7)
    for l in range(DEPTH):
        for t in range(TT):
            for half in range(2):
                take((l, "xT1", t, half), "xT")
        for i in range(4):
            take((l, "conv_in", i), "mm")
        for g in GROUPS:
            for t in range(TT):
                take((l, "qk", g, t), "mm")
                take((l, "qkT", g, t), "tr")
            for t in range(TT):
                take((l, "v", g, t), "mm")
        for i in range(NSTEP):
            if i < NTILE:
                g, hp, t, h = TILES[i]
                for c in range(2 if g == "A" else 1):
                    take((l, "score", i, c), "mm")
                take((l, "probT", i), "tr")
                if h == 0:
                    take((l, "o", i // 2), "o")
            for f in range(2):
                if i == SUBLN_STEP:
                    take((l, "mean", f), "mm")
                if i == ROOT_STEP:
                    take((l, "var", f), "mm")
        for step in range(NSTEP):
            if ada_at(l, step - 1) is not None:
                m, u = ADA_LATER[l][ada_at(l, step - 1)]
                take((m, "mod", u), 7)
            for j in leaves(step):
                take((l, "oT", j), 7)
            if ada_at(l, step) is not None:
                m, u = ADA_LATER[l][ada_at(l, step)]
                take((m, "ada", u), 7)
        for t in range(TT):
            for n in range(2):
                take((l, "out", t, n), "mm")
        for t in range(TT):
            for half in range(2):
                take((l, "xT2", t, half), "xT")
        take((l, "logits"), 7)
        for n, (m, u) in enumerate(ADA_NEXT[l]):
            if n == NORM1_UNITS // 2:
                take((l, "rank"), 5)
            take((m, "ada", u), "mm")
        if not ADA_NEXT[l]:
            take((l, "rank"), 5)
        for n, (m, u) in enumerate(ADA_NEXT[l]):
            take((m, "mod", u), (3, 4, 6, 3)[n])
        take((l, "lists"), 7)
        for b in range(7):
            at[(l, "exp", b)] = (b, used[b])
            used[b] += NE
    return at


def program(nc, a):
    bank_of = plan_banks()
    ctx = ExitStack()
    with ctx:
        def sb(name, shape, dt=F32):
            return ctx.enter_context(nc.sbuf_tensor(name, shape, dt))

        def sem(name):
            return ctx.enter_context(nc.semaphore(name))

        def dram(name, shape, dt=F32):
            return nc.dram_tensor(name, shape, dt, kind="Internal").ap()

        xn2_d = [dram(f"xn2_d{l}", (S, D)) for l in range(DEPTH)]
        yexp_d = [dram(f"yexp_d{l}", (2 * S, D)) for l in range(DEPTH)]

        ps = ctx.enter_context(nc.psum_tensor("ps", [P, 8, 512], F32))

        ring = sb("ring", [P, SLOTS, KD, 512])
        x = sb("x", [P, TT, D])
        gate = sb("gate", [P, 2, D])
        hT = sb("hT", [P, KD, S])
        yT = hT
        arena = sb("arena", [P, 9216])
        xs = arena[:, 0:TT * D].rearrange("p (t d) -> p t d", t=TT)
        qkT = {g: arena[:, 2048 * i:2048 * i + 2048].rearrange("p (f s) -> p f s", f=4) for i, g in enumerate(GROUPS)}
        v = {g: arena[:, 6144 + 1024 * i:7168 + 1024 * i].rearrange("p (t c) -> p t c", t=TT) for i, g in enumerate(GROUPS)}
        xg = [arena[:, D * j:D * j + D] for j in range(2)]
        xgT = [arena[:, 2048 + D * j:2048 + D * j + D].rearrange("p (k s) -> p k s", k=KD) for j in range(2)]
        yexp = [arena[:, 4096 + D * j:4096 + D * j + D] for j in range(2)]
        sil = [arena[:, 6144 + DE * j:6144 + DE * j + DE] for j in range(2)]
        hid = [arena[:, 7168 + DE * j:7168 + DE * j + DE] for j in range(2)]
        hidT = [arena[:, 8192 + DE * j:8192 + DE * j + DE].rearrange("p (c s) -> p c s", c=KE) for j in range(2)]
        yA = v["D"].rearrange("p t c -> p (t c)").rearrange("p (j c) -> p j c", c=P)
        masks = sb("masks", [P, 2, S])
        bias_t = [qkT[g].rearrange("p f s -> p (f s)") for g in "DA"]
        probs = sb("probs", [P, NPROB, S])
        prob = [probs[:, i, :] for i in range(NPROB)]
        probsT = sb("probsT", [P, 2, TT, P])
        probT = [probsT[:, i] for i in range(2)]
        z = sb("z", [P, 2, S + 2 * HALO])
        tmp = sb("tmp", [P, 2, S])
        yrow = [(arena[:, 4 * D:5 * D], arena[:, 5 * D:6 * D]), (arena[:, 6 * D:7 * D], arena[:, 7 * D:8 * D]),
                tuple(probs[:, 2 * k:2 * k + 2, :].rearrange("p a s -> p (a s)") for k in range(2)),
                (probsT[:, :, :, :].rearrange("p a t q -> p (a t q)"), tmp[:, :, :].rearrange("p a s -> p (a s)"))]
        ytok = sb("ytok", [P, P])
        cst = sb("cst", [P, NCONST])
        C = {k: cst[:, C_AT[k]:C_AT[k] + w] for k, w in CONSTS.items()}
        ca = sb("ca", [P, KD])
        csil = sb("csil", [P, KD])
        ca_rep = sb("ca_rep", [P, KD, 32])
        modb = sb("modb", [P, DEPTH * NMOD, KD])
        gcol = sb("gcol", [P, 2, DEPTH, KD])
        modc = sb("modc", [P, 4, KD])
        lamrow = probT[0][:, 0, :]
        lam = probT[0][:, 1, 0:2 * DIFF]
        neglam = sb("neglam", [P, 4])
        subg = sb("subg", [P, HD])
        convw = sb("convw", [P, 2, TAPS])
        convp = sb("convp", [P, 3, 2])
        ssum = sb("ssum", [P, TT])
        rstd = sb("rstd", [P, TT])
        coef = sb("coef", [P, 2])
        oss = sb("oss", [P, 2 * NA0])
        mx = sb("mx", [P, NMAP])
        negm = sb("negm", [P, NMAP])
        lsum = sb("lsum", [P, NMAP])
        rinv = sb("rinv", [P, NMAP])
        wr = sb("wr", [P, KD, NLOG])
        lg = z[:, 0, HALO:HALO + TT * NLOG].rearrange("p (t e) -> p t e", t=TT)
        lem = z[:, 1, HALO:HALO + TT * NE].rearrange("p (t e) -> p t e", t=TT)
        rt = z[:, 0, 200:280]
        top8 = z[:, 0, 300:332].rearrange("p (t n) -> p t n", t=TT)
        idx8 = sb("idx8", [P, TT, 8], U32)
        hot = prob[0][:, 0:2 * TT * NE].rearrange("p (k t e) -> p k t e", k=2, t=TT)
        hots5 = prob[1][:, 0:TT * NE + NE]
        hots = hots5[:, 0:TT * NE].rearrange("p (t e) -> p t e", t=TT)
        sums = prob[3][:, 0:TT * NE + NE].rearrange("p (t e) -> p t e", t=TT + 1)
        rkc = prob[1][:, 256:256 + TT * NE + NE]
        rk = rkc[:, 0:TT * NE].rearrange("p (t e) -> p t e", t=TT)
        hotr = prob[2][:, 0:2 * TT * NE].rearrange("p (k t e) -> p k t e", k=2, t=TT)
        over = sb("over", [P, DEPTH], I32)
        wide = [sb(f"wide{l}", [1, 2], I32) for l in range(DEPTH)]
        widef = sb("widef", [1, NE + 2])
        gates = sb("gates", [P, 2, TT])
        slot_hot = hT[:, 0:2, :].rearrange("p a (n r) -> p (a n) r", r=P)
        slot_val = hT[:, 2:4, :].rearrange("p a (n r) -> p (a n) r", r=P)
        dil = masks[:, :, :].rearrange("p a s -> p (a s)")[:, 0:2 * S - P]
        qpad = {"A": [yT[:, 0, P * n:P * n + P] for n in range(4)], "D": [yT[:, 1, P * n:P * n + P] for n in range(2)],
                "B": [masks[:, 0, P * n:P * n + P] for n in range(2)]}
        lst = masks[:, 0, 0:P].bitcast(I32)
        gidx = masks[:, 0, P:2 * P].bitcast(I32)
        gcolumn = sb("gcolumn", [P, 1], I32)
        scolumn = sb("scolumn", [P, 1], I32)

        slot_in = [sem(f"slot_in{s}") for s in range(SLOTS)]
        filled = [sem(f"bank_filled{b}") for b in range(8)]
        drained = [sem(f"bank_drained{b}") for b in range(8)]
        consts_in, x_in = sem("consts_in"), sem("x_in")
        params_in = sem("params_in")
        table_in = sem("table_in")
        silu_ready, ca_ready = sem("silu_ready"), sem("ca_ready")
        dve_chain, pool_chain = sem("dve_chain"), sem("pool_chain")
        ada_in = sem("ada_in")
        mod_ready = sem("mod_ready")
        sq_summed = sem("sq_summed")
        sq_ready = sem("sq_ready")
        oss_ready, oss_root = sem("oss_ready"), sem("oss_root")
        xs_ready = sem("xs_ready")
        halo_ready = sem("halo_ready")
        sig_ready = sem("sig_ready")
        rot_ready = sem("rot_ready")
        max_ready = sem("max_ready")
        exp_ready = sem("exp_ready")
        mix_ready = sem("mix_ready")
        pv_done = sem("pv_done")
        yA_ready = sem("yA_ready")
        bias_in, bias_ready = sem("bias_in"), sem("bias_ready")
        conv_part = sem("conv_part")
        conv_done = [sem(f"conv_done{f}") for f in range(2)]
        stat_ready = sem("stat_ready")
        pad_zeroed, pad_ready = sem("pad_zeroed"), sem("pad_ready")
        log_ready = sem("log_ready")
        norm_ready = sem("norm_ready")
        conv_ready = sem("conv_ready")
        mixed = sem("mixed")
        xn_out = sem("xn_out")
        rin_ready, rexp_ready = sem("rin_ready"), sem("rexp_ready")
        hots_ready = sem("hots_ready")
        slots_ready = sem("slots_ready")
        gidx_ready = sem("gidx_ready")
        xg_in = [sem(f"xg_in{j}") for j in range(2)]
        yrow_out = [sem(f"yrow_out{j}") for j in range(2)]
        yrow_in = [sem(f"yrow_in{t}") for t in range(TT)]
        over_ready = sem("over_ready")
        over_w = [sem(f"over_weights{l}") for l in range(DEPTH)]
        over_xg = [sem(f"over_tokens{l}") for l in range(DEPTH)]
        over_pe = [sem(f"over_pe{l}") for l in range(DEPTH)]
        over_act = [sem(f"over_act{l}") for l in range(DEPTH)]
        over_dve = [sem(f"over_dve{l}") for l in range(DEPTH)]
        over_out = [sem(f"over_rows{l}") for l in range(DEPTH)]
        half_ready, comb_ready = sem("half_ready"), sem("comb_ready")
        x_done = sem("x_done")
        rin_lam, rexp_lam = sem("lambda_in"), sem("lambda_exp")
        gfin_in = sem("gfin_in")
        fin_ready, out_done = sem("fin_ready"), sem("out_done")
        N_PARAMS, N_TABLES = 6, 9

        def bank(key):
            return ps[:, bank_of[key][0], :]

        def bank4(key):
            return bank(key).rearrange("p (a s) -> p a s", a=4)

        def fills(ins, key):
            ins.then_inc(filled[bank_of[key][0]], 1)

        def drains(ins, key):
            ins.then_inc(drained[bank_of[key][0]], 1)

        def await_filled(eng, key):
            eng.wait_ge(filled[bank_of[key][0]], bank_of[key][1] + 1)

        def await_drained(eng, key):
            eng.wait_ge(drained[bank_of[key][0]], bank_of[key][1] + 1)

        def await_free(eng, key):
            if bank_of[key][1]:
                eng.wait_ge(drained[bank_of[key][0]], bank_of[key][1])

        def slot(unit):
            return ring[:, unit % SLOTS, :, :]

        def await_unit(eng, unit):
            eng.wait_ge(slot_in[unit % SLOTS], 16 * (unit // SLOTS + 1))

        def last_use(unit):
            kind, l, u = ORDER[unit]
            if kind == "ada":
                return l, "ada", u
            if kind == "win":
                return (l, "conv_in", 3) if u == 0 else (l, "qk" if u % 2 else "v", GROUPS[(u - 1) // 2], TT - 1)
            return (l, "out", TT - 1, u) if kind == "wout" else None

        def wide_words(eng, l):
            eng.wait_ge(over_ready, l + 1)
            return [eng.value_load(wide[l][0:1, j:j + 1], min_val=0, max_val=2 ** HE - 1) for j in range(2)]

        def by_width(eng, words, it, j, body):
            with eng.If(((words[j] >> it) & 1) > 0):
                body(P)
            with eng.Else():
                body(HALF)

        def on_overflow(eng, l):
            eng.wait_ge(over_ready, l + 1)
            return eng.If(eng.value_load(over[0:1, l:l + 1], min_val=0, max_val=1) > 0)

        maps = [(i, c) for i, tile in enumerate(TILES) for c in range(2 if tile[0] == "A" else 1)]
        map_no = {m: n for n, m in enumerate(maps)}
        NQK = len(GROUPS) * TT

        def prob_of(n):
            return prob[n % NPROB]

        def await_prob(eng, l, n):
            n -= NPROB
            if n >= NQK:
                await_filled(eng, (l, "probT", maps[n - NQK][0]))
            elif n >= 0:
                await_filled(eng, (l, "qkT", GROUPS[n // TT], n % TT))

        def expert_bank(l, b):
            return bank_of[(l, "exp", b)][1]

        HE = NE // 2

        def route(dve, link, mod_out, l):
            key = (l, "logits")
            await_filled(dve, key)
            drains(dve.tensor_copy(lg.rearrange("p t e -> p (t e)"), bank(key)[:, 0:TT * NLOG]), key)
            await_drained(dve, key)
            gl = lg[:, :, 0:NG]
            W = 2 * (S + 2 * HALO)

            def r3(first, n=NG):
                return rt[:, first:first + TT * n].rearrange("p (t n) -> p t n", t=TT)

            def spread(first, n):
                return view(z, 200 + first, [[W, P], [1, TT], [0, n]])

            link(dve.memset(sums[:, 0, :], 0.0))
            link(dve.memset(hots5[:, TT * NE:], 0.0))
            diff, dv, gmax, pgrp = 0, 16, 20, 24
            eq, vmax, hotg, e01 = 28, 44, 48, 64
            link(dve.tensor_reduce(rt[:, gmax:gmax + TT], gl, AX_X, ALU.max))
            dve.tensor_tensor(r3(diff), gl, spread(gmax, NG), ALU.subtract).then_inc(rin_ready, 1)
            link(dve.tensor_tensor(r3(eq), gl, spread(gmax, NG), ALU.is_equal))
            link(dve.tensor_tensor(r3(eq), r3(eq), view(cst, C_AT["first"], [[NCONST, P], [0, TT], [1, NG]]), ALU.mult))
            link(dve.tensor_reduce(rt[:, vmax:vmax + TT], r3(eq), AX_X, ALU.max))
            link(dve.tensor_tensor(r3(hotg), r3(eq), spread(vmax, NG), ALU.is_equal))
            link(dve.tensor_scalar(rt[:, hotg:hotg + 16], rt[:, hotg:hotg + 16], -1.0, -NEG, ALU.add, ALU.mult))
            for t in range(TT):
                last = dve.tensor_tensor(lem[:, t, :].rearrange("p (g e) -> p g e", g=NG),
                                         lg[:, t, NG:].rearrange("p (g e) -> p g e", g=NG),
                                         view(z, 200 + hotg + NG * t, [[W, P], [1, NG], [0, EPG]]), ALU.add)
            link(last)
            for t in range(TT):
                last = dve.max(top8[:, t, :], lem[:, t, :])
            link(last)
            for t in range(TT):
                last = dve.max_index(idx8[:, t, :], top8[:, t, :], lem[:, t, :])
            link(last)
            dve.tensor_tensor(rt[:, dv:dv + TT], top8[:, :, 1], top8[:, :, 0], ALU.subtract).then_inc(rin_ready, 1)
            e2 = rt[:, e01:e01 + 2 * TT].rearrange("p (k t) -> p k t", k=2)
            link(dve.tensor_copy(e2, idx8[:, :, 0:2].rearrange("p t k -> p k t")))
            iota = view(cst, C_AT["iota"], [[NCONST, P], [0, TT], [1, NE]])
            for k in range(2):
                last = dve.tensor_tensor(hot[:, k], iota, spread(e01 + TT * k, NE), ALU.is_equal)
            link(last)
            link(dve.tensor_tensor(hots, hot[:, 0], hot[:, 1], ALU.add))
            link(dve.tensor_copy(sums[:, 1, :], hots[:, 0, :]))
            for t in range(1, TT):
                ins = dve.tensor_tensor(sums[:, t + 1, :], sums[:, t, :], hots[:, t, :], ALU.add)
                if t < TT - 1:
                    link(ins)
            ins.then_inc(hots_ready, 1)
            dve.wait_ge(rexp_ready, 2 * (l + 1))
            link(dve.tensor_reduce(rt[:, pgrp:pgrp + TT], r3(diff), AX_X, ALU.add))
            link(dve.tensor_scalar(gates[:, 0, :], rt[:, dv:dv + TT], 1.0, None, ALU.add))
            link(dve.tensor_tensor(gates[:, 0, :], gates[:, 0, :], rt[:, pgrp:pgrp + TT], ALU.mult))
            link(dve.reciprocal(gates[:, 0, :], gates[:, 0, :]))
            link(dve.tensor_tensor(gates[:, 1, :], gates[:, 0, :], rt[:, dv:dv + TT], ALU.mult))
            key = (l, "rank")
            await_filled(dve, key)
            drains(dve.tensor_copy(rkc, bank(key)[:, 0:TT * NE + NE]), key)
            await_drained(dve, key)
            for k in range(2):
                last = dve.tensor_tensor(hotr[:, k], hot[:, k], rk, ALU.mult)
            link(last)
            rank, blk = rt[:, 0:8], rt[:, 72:80]
            link(dve.tensor_reduce(rank, hotr.rearrange("p k t e -> p (k t) e"), AX_X, ALU.add))
            link(dve.tensor_scalar(blk, rank, float(CAP), None, ALU.is_ge))
            for b in range(2, NBLK):
                link(dve.scalar_tensor_tensor(blk, rank, float(CAP * b), blk, ALU.is_ge, ALU.add))
            link(dve.scalar_tensor_tensor(rank, blk, -float(CAP), rank, ALU.mult, ALU.add))
            dve.tensor_tensor(slot_hot, view(cst, C_AT["iota"], [[NCONST, P], [0, 2 * TT], [1, P]]),
                              view(z, 200, [[W, P], [1, 2 * TT], [0, P]]), ALU.is_equal)
            beq = rt[:, 8:8 + 2 * TT * NBLK]
            link(dve.tensor_tensor(beq.rearrange("p (n b) -> p n b", b=NBLK), view(cst, C_AT["iota"], [[NCONST, P], [0, 2 * TT], [1, NBLK]]),
                                   view(z, 200 + 72, [[W, P], [1, 2 * TT], [0, NBLK]]), ALU.is_equal))
            link(dve.tensor_tensor(hotr.rearrange("p k t e -> p (k t) e"), hot.rearrange("p k t e -> p (k t) e"),
                                   view(cst, C_AT["ids"], [[NCONST, P], [1, 2 * TT], [0, NE]]), ALU.mult))
            for b in range(NBLK):
                last = dve.tensor_tensor(slot_val[:, :, NE * b:NE * b + NE], hotr.rearrange("p k t e -> p (k t) e"),
                                         view(z, 200 + 8 + b, [[W, P], [NBLK, 2 * TT], [0, NE]]), ALU.mult)
            last.then_inc(slots_ready, 1)
            link(dve.tensor_scalar(widef[:, 0:NE], rkc[0:1, TT * NE:], HALF + 0.5, None, ALU.is_ge))
            link(dve.tensor_tensor(widef[:, 0:NE], widef[:, 0:NE], C["bit"][0:1, :], ALU.mult))
            link(dve.tensor_reduce(widef[:, NE:NE + 2], widef[:, 0:NE].rearrange("p (i j) -> p j i", j=2), AX_X, ALU.add))
            link(dve.tensor_copy(wide[l][:, :], widef[:, NE:NE + 2]))
            link(dve.tensor_reduce(rt[:, 40:41], rkc[:, TT * NE:], AX_X, ALU.max))
            dve.tensor_scalar(over[:, l:l + 1], rt[:, 40:41], CAP + 0.5, None, ALU.is_ge).then_inc(over_ready, 1)
            for m, u in ADA_NEXT[l][:2]:
                mod_out(m, u)
            key = (l, "lists")
            await_filled(dve, key)
            lists = bank(key)[:, 0:P]
            link(dve.tensor_scalar(slot_hot[:, 0, :], lists, 0.5, NO_SLOT + 1.0, ALU.is_lt, ALU.mult))
            drains(dve.scalar_tensor_tensor(lst, lists, -1.0, slot_hot[:, 0, :], ALU.add, ALU.add), key)
            await_drained(dve, key)
            link(dve.tensor_scalar(gidx, lst, S, -S, ALU.is_ge, ALU.mult))
            dve.tensor_tensor(gidx, lst, gidx, ALU.add).then_inc(gidx_ready, 1)
            for m, u in ADA_NEXT[l][2:]:
                mod_out(m, u)

        def experts_dve(dve, l):
            def at(b, e):
                return e + expert_bank(l, b)

            def expert_tokens(e, j):
                dve.wait_ge(filled[4], at(4, e) + 1)
                if not isinstance(e, int) or e >= 2:
                    dve.wait_ge(filled[1], at(1, e) - 1)
                for q in range(4):
                    k = 4 + q
                    last = dve.tensor_scalar(xgT[j][:, k, :], ps[:, 4, P * q:P * q + P], modc[:, 3, k:k + 1],
                                             modc[:, 2, k:k + 1], ALU.mult, ALU.add)
                last.then_inc(drained[4], 1)

            def expert_hidden(e, it, j):
                def body(w):
                    dve.wait_ge(filled[1], at(1, e) + 1)
                    dve.wait_ge(drained[0], at(0, e) + 1)
                    if not isinstance(e, int) or e >= 2:
                        dve.wait_ge(filled[2], at(2, e) - 1)
                    dve.tensor_tensor(hid[j][0:w, :], ps[P - w:P, 1, :], sil[j][0:w, :], ALU.mult).then_inc(drained[1], 1)
                by_width(dve, words, it, j, body)

            def expert_rows(e, it, j):
                def body(w):
                    dve.wait_ge(filled[6], at(6, e) + 1)
                    if not isinstance(it, int) or it >= 1 or l:
                        dve.wait_ge(yrow_out[j], 16 * it + 16 * l * HE)
                    dve.tensor_copy(yexp[j][0:w, 512:D], ps[P - w:P, 6, :]).then_inc(drained[6], 1)
                by_width(dve, words, it, j, body)

            words = wide_words(dve, l)
            expert_tokens(0, 0)
            expert_hidden(0, 0, 0)
            expert_tokens(1, 1)
            expert_hidden(1, 0, 1)
            expert_rows(0, 0, 0)
            expert_tokens(2, 0)
            expert_hidden(2, 1, 0)
            expert_rows(1, 0, 1)
            expert_tokens(3, 1)
            with dve.Fori(1, HE - 1) as it:
                expert_hidden(2 * it + 1, it, 1)
                expert_rows(2 * it, it, 0)
                expert_tokens(2 * it + 2, 0)
                expert_hidden(2 * it + 2, it + 1, 0)
                expert_rows(2 * it + 1, it, 1)
                expert_tokens(2 * it + 3, 1)
            expert_hidden(NE - 1, HE - 1, 1)
            expert_rows(NE - 2, HE - 1, 0)
            expert_rows(NE - 1, HE - 1, 1)
            with on_overflow(dve, l):
                with dve.Fori(0, NE * (NBLK - 1)) as n:
                    dve.wait_ge(over_pe[l], 4 * n + 1)
                    for q in range(4):
                        k = 4 + q
                        last = dve.tensor_scalar(xgT[0][:, k, :], ps[:, 4, P * q:P * q + P], modc[:, 3, k:k + 1],
                                                 modc[:, 2, k:k + 1], ALU.mult, ALU.add)
                    last.then_inc(over_dve[l], 1)
                    dve.wait_ge(over_act[l], 4 * n + 2)
                    dve.tensor_tensor(hid[0], ps[:, 1, :], sil[0], ALU.mult).then_inc(over_dve[l], 1)
                    dve.wait_ge(over_pe[l], 4 * n + 4)
                    dve.tensor_copy(yexp[0][:, 512:D], ps[:, 6, :]).then_inc(over_dve[l], 1)

        block = ctx.enter_context(nc.Block())

        @block.sync
        def _(sp):
            def load(unit, dst, src):
                old = unit - SLOTS
                if old >= 0:
                    key = last_use(old)
                    if key:
                        await_filled(sp, key)
                    else:
                        _, lo, e3 = ORDER[old]
                        e, c = divmod(e3, 3)
                        b = (0, 1, 6)[c]
                        sp.wait_ge(filled[b], expert_bank(lo, b) + e + 1)
                sp.dma_start(dst, src).then_inc(slot_in[unit % SLOTS], 16)

            def load_ada(l, u):
                unit = UNIT["ada", l, u]
                load(unit, slot(unit), a["w_ada"][l].rearrange("(p k) n -> p k n", k=KD)[:, :, 512 * u:512 * u + 512])

            sp.dma_start(ca[:, :], a["c"].rearrange("b (p k) -> (b p) k", k=KD)).then_inc(consts_in, 16)
            sp.dma_start(cst[:, :], a["consts"]).then_inc(consts_in, 16)
            for u in range(NORM1_UNITS):
                load_ada(0, u)
                if u == 1:
                    sp.dma_start(x[:, :, :], a["x"].rearrange("b (t p) d -> p (b t) d", p=P)).then_inc(x_in, 16)
            for l in range(DEPTH):
                for n, (c0, w) in enumerate(WIN_COLS):
                    unit = UNIT["win", l, n]
                    if l and n == 2:
                        sp.wait_ge(yrow_in[TT - 1], 32 * l)
                    load(unit, slot(unit)[:, :, 0:w], a["w_in"][l].rearrange("(p k) n -> p k n", k=KD)[:, :, c0:c0 + w])
                for m, u in ADA_LATER[l]:
                    load_ada(m, u)
                for n in range(2):
                    unit = UNIT["wout", l, n]
                    load(unit, slot(unit), a["w_out"][l].rearrange("(k p) n -> p k n", p=P)[:, :, 512 * n:512 * n + 512])
                for m, u in ADA_NEXT[l]:
                    load_ada(m, u)
                w3 = [a[name][l].rearrange("(i j) (p k) n -> i j p (k n)", j=2, p=P)
                      for name in ("w_exp_gate", "w_exp_up", "w_exp_down")]
                for j in range(2):
                    for c in range(3):
                        unit = UNIT["exp", l, 3 * j] + c
                        load(unit, slot(unit).rearrange("p k n -> p (k n)"), w3[c][0, j])
                with sp.Fori(1, HE) as it:
                    for j in range(2):
                        for c, b in enumerate((0, 1, 6)):
                            unit = UNIT["exp", l, 3 * j] + c
                            sp.wait_ge(filled[b], 2 * it + (expert_bank(l, b) + j - 1))
                            sp.dma_start(slot(unit).rearrange("p k n -> p (k n)"), w3[c][it, j])\
                                .then_inc(slot_in[unit % SLOTS], 16)
                with on_overflow(sp, l):
                    sp.wait_ge(filled[6], expert_bank(l, 6) + NE)
                    sp.wait_ge(filled[1], expert_bank(l, 1) + NE)
                    flat = [a[name][l].rearrange("e (p k) n -> e p (k n)", p=P) for name in ("w_exp_gate", "w_exp_up", "w_exp_down")]
                    with sp.Fori(0, NBLK - 1) as b, sp.Fori(0, NE) as e:
                        sp.wait_ge(over_xg[l], 16 * NE * b + 16 * e + 16)
                        for c in range(3):
                            sp.dma_start(ring[:, c, :, :].rearrange("p k n -> p (k n)"), flat[c][e]).then_inc(over_w[l], 16)
                    sp.wait_ge(over_pe[l], 4 * NE * (NBLK - 1))

            for t in range(TT):
                sp.wait_ge(fin_ready, t + 1)
                sp.dma_start(a["out"].rearrange("b (t p) d -> t p (b d)", p=P)[t], x[:, t, :]).then_inc(out_done, 16)
            sp.wait_ge(out_done, 16 * TT)

        @block.gpsimd
        def _(pool):
            chain = [0]

            def link(ins):
                chain[0] += 1
                ins.then_inc(pool_chain, 1)
                pool.wait_ge(pool_chain, chain[0])

            last_token, last_row = pool.to_reg(S - 1), pool.to_reg(2 * S - 1)
            pool.memset(z[:, :, 0:HALO], 0.0).then_inc(halo_ready, 1)
            pool.memset(z[:, :, HALO + S:], 0.0).then_inc(halo_ready, 1)

            for l in range(DEPTH):
                if l:
                    pool.wait_ge(x_done, TT * l)
                else:
                    await_unit(pool, NORM1_UNITS - 1)
                for n in range(2):
                    row = (3 * n + 2) * D
                    pool.dma_start(gate[:, n, :], view(a["b_ada"], l * NMOD * D + row, [[0, P], [1, D]])).then_inc(params_in, 16)
                pool.dma_start(lamrow, view(a["diff_lambda"], l * 4 * DIFF, [[0, P], [1, 4 * DIFF]])).then_inc(params_in, 16)
                pool.dma_start(subg[:, :], view(a["diff_subln"], l * HD, [[0, P], [1, HD]])).then_inc(params_in, 16)
                for f in range(2):
                    pool.dma_start(convw[:, f, :], a["conv_dw"][l, P * f:P * f + P, :])\
                        .then_inc(params_in, 16)
                for n, name in enumerate(("conv_b", "conv_norm_g", "conv_norm_b")):
                    pool.dma_start(convp[:, n, :], view(a[name], l * GW, [[1, P], [P, 2]]), allow_slow_non_contiguous=True).then_inc(table_in, 16)
                pool.dma_start(wr[:, :, 0:NG], a["w_router_group"][l].rearrange("(p k) g -> p k g", k=KD)).then_inc(table_in, 16)
                for g in range(NG):
                    pool.dma_start(wr[:, :, NG + EPG * g:NG + EPG * g + EPG],
                                   a["w_router_expert"][l, g].rearrange("(p k) e -> p k e", k=KD)).then_inc(table_in, 16)
                pool.dma_start(dil[:, :], a["dilation"]).then_inc(table_in, 16)

                pool.wait_ge(params_in, 16 * N_PARAMS * (l + 1))
                pool.wait_ge(table_in, 16 * N_TABLES * (l + 1))
                await_drained(pool, (l, "conv_in", 3))
                await_filled(pool, (l, "v", "B", TT - 1))
                acc, part = yT[:, FIRST_F["B"], :], yT[:, FIRST_F["B"] + 1, :]
                link(pool.tensor_scalar(acc, z[:, 1, DVE_TAPS:DVE_TAPS + S], convw[:, 1, DVE_TAPS:DVE_TAPS + 1], None, ALU.mult))
                for k in range(DVE_TAPS + 1, TAPS):
                    link(pool.tensor_scalar(part, z[:, 1, k:k + S], convw[:, 1, k:k + 1], None, ALU.mult))
                    link(pool.tensor_tensor(acc, acc, part, ALU.add))
                pool.wait_ge(conv_part, l + 1)
                total = yT[:, FIRST_F["C"] + 1, :]
                pool.tensor_tensor(total, total, acc, ALU.add).then_inc(conv_done[1], 1)

                rows_b = RPB_H - 1
                for hp in range(2):
                    last = (hp + 1) * NTILE // 3 - 1
                    await_drained(pool, (l, "score", last, hp))
                    for h in range(2):
                        for up in range(2):
                            n = rows_b * GRID_W
                            pool.dma_start(bias_t[hp][GRID_W * up:GRID_W * up + GRID_W, n * h:n * h + n],
                                           a["rpb"][l, 2 * hp + h, :, GRID_W * (1 - up):GRID_W * (1 - up) + n])\
                                .then_inc(bias_in, 16)
                    pool.wait_ge(bias_in, 128 * l + 64 * (hp + 1))
                    for h in range(2):
                        n = rows_b * GRID_W
                        tab = bias_t[hp][:, n * h:n * h + n].rearrange("p (r w) -> p r w", w=GRID_W)
                        cm = view(cst, C_AT["colmask"], [[NCONST, P], [0, rows_b], [1, GRID_W]])
                        link(pool.tensor_scalar(tab, tab, HD ** 0.5, None, ALU.mult))
                        pool.tensor_tensor(tab, tab, cm, ALU.add).then_inc(bias_ready, 1)

                for t in range(TT):
                    for n in range(2):
                        await_drained(pool, (l, "out", t, n))
                        xh = x[:, t, 512 * n:512 * n + 512]
                        pool.tensor_tensor(xh, xh, tmp[:, n, :], ALU.add).then_inc(mixed, 1)
                if l == DEPTH - 1:
                    pool.dma_start(gate[:, 0, :], view(a["g_final"], 0, [[0, P], [1, D]])).then_inc(gfin_in, 16)

                pool.wait_ge(xn_out, 16 * TT * (l + 1))
                await_filled(pool, (l, "xT2", TT - 1, 1))
                for j in range(2):
                    link(pool.memset(xg[j], 0.0))
                pool.wait_ge(gidx_ready, l + 1)

                words = wide_words(pool, l)

                def gather(e):
                    def body(w):
                        if e >= 2:
                            pool.wait_ge(filled[4], expert_bank(l, 4) + e - 1)
                        pool.indirect_dma_start(xg[e % 2][0:w, :], None, xn2_d[l],
                                                bass.IndirectOffsetOnAxis(ap=gidx[0:w, e:e + 1], axis=0),
                                                bounds_check=last_token, oob_is_err=False).then_inc(xg_in[e % 2], 16)
                    by_width(pool, words, e // 2, e % 2, body)

                def scatter(e):
                    def body(w):
                        pool.wait_ge(drained[5], expert_bank(l, 5) + e + 1)
                        pool.wait_ge(drained[6], expert_bank(l, 6) + e + 1)
                        pool.indirect_dma_start(yexp_d[l], bass.IndirectOffsetOnAxis(ap=lst[0:w, e:e + 1], axis=0),
                                                yexp[e % 2][0:w, :], None, bounds_check=last_row, oob_is_err=False)\
                            .then_inc(yrow_out[e % 2], 16)
                    by_width(pool, words, e // 2, e % 2, body)

                for e in range(2):
                    gather(e)
                for e in range(NE):
                    if e + 2 < NE:
                        gather(e + 2)
                    scatter(e)
                with on_overflow(pool, l):
                    for j in range(2):
                        pool.wait_ge(yrow_out[j], 16 * HE * (l + 1))
                    with pool.Fori(0, NE * (NBLK - 1)) as n:
                        pool.tensor_copy(gcolumn[:, :], gidx[:, bass.ds(n + NE, 1)])
                        pool.drain()
                        pool.indirect_dma_start(xg[0], None, xn2_d[l], bass.IndirectOffsetOnAxis(ap=gcolumn[:, :], axis=0),
                                                bounds_check=last_token, oob_is_err=False).then_inc(over_xg[l], 16)
                        pool.wait_ge(over_act[l], 4 * n + 4)
                        pool.wait_ge(over_dve[l], 3 * n + 3)
                        pool.tensor_copy(scolumn[:, :], lst[:, bass.ds(n + NE, 1)])
                        pool.drain()
                        pool.indirect_dma_start(yexp_d[l], bass.IndirectOffsetOnAxis(ap=scolumn[:, :], axis=0),
                                                yexp[0], None, bounds_check=last_row, oob_is_err=False)\
                            .then_inc(over_out[l], 16)
                        pool.wait_ge(over_out[l], 16 * n + 16)
                for t in range(TT // 2):
                    pool.wait_ge(comb_ready, TT * l + t + 1)
                    pool.tensor_tensor(x[:, t, :], x[:, t, :], yrow[t][0], ALU.add).then_inc(x_done, 1)

        @block.tensor
        def _(pe):
            ident = C["ident"]

            def product(out, lhs, rhs, n=KD):
                for k in range(n):
                    last = pe.matmul(out, lhs(k), rhs(k), start=(k == 0), stop=(k == n - 1))
                return last

            def transposed_x(l, which, tiles=range(TT)):
                for t in tiles:
                    pe.wait_ge(xs_ready, TT * (2 * l + which - 1) + t + 1)
                    for half in range(2):
                        key = (l, f"xT{which}", t, half)
                        await_free(pe, key)
                        for q in range(4):
                            k = 4 * half + q
                            last = pe.transpose(bank4(key)[:, q, :], xs[:, t, k:D:KD], ident)
                        fills(last, key)

            def ada(l, u):
                key, unit = (l, "ada", u), UNIT["ada", l, u]
                await_unit(pe, unit)
                await_free(pe, key)
                for r in range(2):
                    for q in range(4):
                        k = 4 * r + q
                        last = pe.matmul(bank(key)[32 * q:32 * q + 32, :], ca_rep[:, k, :], slot(unit)[:, k, :],
                                         start=(r == 0), stop=(r == 1), tile_position=(0, 32 * q))
                fills(last, key)

            def mod(l, u, part):
                key = (l, "mod", u)
                await_drained(pe, (l, "ada", u))
                await_free(pe, key)
                if u // 2 % 3 == 2:
                    fills(pe.matmul(bank(key), C["ones"], tmp[:, part, :], start=True, stop=True), key)
                    return
                p0 = HALF * (u % 2)
                for k in range(KD):
                    last = pe.matmul(bank(key)[p0:p0 + HALF, k:k + 1], tmp[:, part, k:512:KD], C["ones"][:, 0:1],
                                     start=True, stop=True, tile_position=(0, p0))
                fills(last, key)

            pe.wait_ge(consts_in, 32)
            pe.wait_ge(ca_ready, 1)
            for u in range(NORM1_UNITS + 1):
                if u < NORM1_UNITS:
                    ada(0, u)
                if u:
                    mod(0, u - 1, (u - 1) % 2)
            for l in range(DEPTH):
                transposed_x(l, 1)
                await_drained(pe, (l, "xT1", TT - 1, 0))
                await_drained(pe, (l, "xT1", TT - 1, 1))

                unit = UNIT["win", l, 0]
                await_unit(pe, unit)
                for i in range(4):
                    key = (l, "conv_in", i)
                    await_free(pe, key)
                    c0 = GW * (1 - i % 2) + P * (i // 2)
                    fills(product(bank(key), lambda k: slot(unit)[:, k, c0:c0 + P], lambda k: hT[:, k, :]), key)

                def qk_turn(g, t):
                    key = (l, "qkT", g, t)
                    n = GROUPS.index(g) * TT + t
                    pe.wait_ge(rot_ready, NQK * l + n + 1)
                    await_free(pe, key)
                    for f in range(4):
                        last = pe.transpose(bank4(key)[:, f, :], prob_of(n)[:, P * f:P * f + P], ident)
                    fills(last, key)

                for gi_, g in enumerate(GROUPS):
                    unit = UNIT["win", l, 1 + 2 * gi_]
                    await_unit(pe, unit)
                    for t in range(TT):
                        key = (l, "qk", g, t)
                        await_free(pe, key)
                        fills(product(bank(key), lambda k: hT[:, k, P * t:P * t + P], lambda k: slot(unit)[:, k, :]), key)
                        if t >= 2:
                            qk_turn(g, t - 2)
                    unit += 1
                    await_unit(pe, unit)
                    for t in range(TT):
                        key = (l, "v", g, t)
                        await_free(pe, key)
                        fills(product(bank(key)[:, 0:GW], lambda k: hT[:, k, P * t:P * t + P], lambda k: slot(unit)[:, k, 0:GW]), key)
                        if t < 2:
                            qk_turn(g, t + 2)

                def scores(i):
                    g, hp, t, h = TILES[i]
                    if i % (NTILE // 3) == 0:
                        await_drained(pe, (l, "qkT", g, TT - 1))
                    for c in range(2 if g == "A" else 1):
                        key = (l, "score", i, c)
                        pe.wait_ge(pad_ready, NMAP * l + map_no[(i, c)] + 1)
                        await_free(pe, key)
                        fills(pe.matmul(bank(key), qpad[g][2 * h + c if g == "A" else h], qkT[g][:, 2 + hp, :],
                                        start=True, stop=True), key)

                def turn(i):
                    g = TILES[i][0]
                    if g == "A":
                        pe.wait_ge(mix_ready, NTILE // 3 * l + i - NTILE // 3 + 1)
                    else:
                        pe.wait_ge(exp_ready, 2 * NTILE // 3 * l + (i if g == "D" else i - NTILE // 3) + 1)
                    key = (l, "probT", i)
                    await_free(pe, key)
                    src = prob_of(NQK + map_no[(i, 0)])
                    for kt in range(TT):
                        last = pe.transpose(bank4(key)[:, kt, :], src[:, P * kt:P * kt + P], ident)
                    fills(last, key)

                def attend(i):
                    g, hp, t, h = TILES[i]
                    key = (l, "o", i // 2)
                    if h == 0:
                        await_free(pe, key)
                    await_drained(pe, (l, "probT", i))
                    if i % (NTILE // 3) == 0:
                        await_drained(pe, (l, "v", g, TT - 1))
                    c0 = HD * (2 * hp + h)
                    last = product(bank(key)[:, HD * h:HD * h + HD], lambda k: probT[i % 2][:, k, :],
                                   lambda k: v[g][:, k, c0:c0 + HD], n=TT)
                    if h:
                        fills(last, key)
                    else:
                        last.then_inc(pv_done, 1)

                def leave(j):
                    key = (l, "oT", j)
                    await_free(pe, key)
                    if NA0 <= j < 2 * NA0:
                        pe.wait_ge(yA_ready, l + 1)
                    else:
                        await_drained(pe, (l, "o", j))
                    src = yA[:, j - NA0, :] if NA0 <= j < 2 * NA0 else ytok[:, :]
                    fills(pe.transpose(bank(key)[:, 0:P], src, ident), key)

                def group_norm(f, stage):
                    if stage == 0:
                        pe.wait_ge(conv_done[f], l + 1)
                    else:
                        pe.wait_ge(stat_ready, 2 * l + f + 1)
                    key = (l, ("mean", "var")[stage], f)
                    await_free(pe, key)
                    src = yT[:, FIRST_F["C"] + f, :] if stage == 0 else tmp[:, f, :]
                    fills(pe.matmul(bank(key), C["groupmean"], src, start=True, stop=True), key)

                for i in range(NSTEP):
                    if i < NTILE:
                        scores(i)
                    if 2 <= i < NTILE + 2:
                        turn(i - 2)
                    if 3 <= i < NTILE + 3:
                        attend(i - 3)
                    if ada_at(l, i - 1) is not None:
                        n = ada_at(l, i - 1)
                        mod(*ADA_LATER[l][n], n % 2)
                    for j in leaves(i):
                        leave(j)
                    if ada_at(l, i) is not None:
                        ada(*ADA_LATER[l][ada_at(l, i)])
                    if SUBLN_STEP <= i < SUBLN_STEP + 2:
                        for f in range(2):
                            group_norm(f, i - SUBLN_STEP)

                def logits(t):
                    key = (l, "logits")
                    if t == 0:
                        await_free(pe, key)
                    for half in range(2):
                        await_drained(pe, (l, "xT2", t, half))
                    last = product(bank(key)[:, NLOG * t:NLOG * t + NLOG], lambda k: hT[:, k, P * t:P * t + P], lambda k: wr[:, k, :])
                    if t == TT - 1:
                        fills(last, key)

                await_drained(pe, (l, "oT", NOUT - 1))
                await_drained(pe, (l, "oT", 2 * NA0 - 1))
                pe.wait_ge(conv_ready, 2 * (l + 1))
                pe.wait_ge(table_in, 16 * N_TABLES * (l + 1))
                for t in range(TT + 2):
                    if t < TT:
                        for n in range(2):
                            unit = UNIT["wout", l, n]
                            if t == 0:
                                await_unit(pe, unit)
                            key = (l, "out", t, n)
                            await_free(pe, key)
                            fills(product(bank(key), lambda k: yT[:, k, P * t:P * t + P], lambda k: slot(unit)[:, k, :]), key)
                    if 1 <= t <= TT:
                        transposed_x(l, 2, [t - 1])
                    if 2 <= t < TT + 2:
                        logits(t - 2)
                half = NORM1_UNITS // 2
                for m, u in ADA_NEXT[l][:half]:
                    ada(m, u)
                key = (l, "rank")
                pe.wait_ge(hots_ready, l + 1)
                await_free(pe, key)
                n = TT * NE + NE
                pe.matmul(bank(key)[:, 0:n], C["ones"], sums.rearrange("p t e -> p (t e)"), start=True, stop=False)
                fills(pe.matmul(bank(key)[:, 0:n], C["before"], hots5, start=False, stop=True), key)
                for n, (m, u) in enumerate(ADA_NEXT[l][:half]):
                    mod(m, u, n)
                for m, u in ADA_NEXT[l][half:]:
                    ada(m, u)
                key = (l, "lists")
                pe.wait_ge(slots_ready, l + 1)
                await_free(pe, key)
                fills(product(bank(key)[:, 0:P], lambda n: slot_hot[:, n, :], lambda n: slot_val[:, n, :], n=2 * TT), key)
                for n, (m, u) in enumerate(ADA_NEXT[l][half:]):
                    mod(m, u, n)

                def bank_e(b):
                    return ps[:, b, :]

                def at(b, e):
                    return e + expert_bank(l, b)

                def await_bank_free(b, e):
                    pe.wait_ge(drained[b], at(b, e))

                def turn_tokens(e, it, j):
                    pe.wait_ge(xg_in[j], 16 * it + 16 * (l * HE + 1))
                    for half in range(2):
                        b = 3 + half
                        await_bank_free(b, e)
                        for q in range(4):
                            k = 4 * half + q
                            last = pe.transpose(bank_e(b).rearrange("p (a s) -> p a s", a=4)[:, q, :], xg[j][:, k:D:KD], ident)
                        last.then_inc(filled[b], 1)

                def await_slot(it, unit):
                    pe.wait_ge(slot_in[unit % SLOTS], 16 * it + 16 * (unit // SLOTS + 1))

                def pair(w, outs, lhs, rhs, n):
                    if w == P:
                        return [product(outs[c], lhs, lambda k: rhs(c, k), n=n) for c in range(2)]
                    for k in range(n):
                        last = [pe.matmul(outs[c][HALF * c:HALF * c + HALF, :], lhs(k)[:, 0:HALF], rhs(c, k),
                                          start=(k == 0), stop=(k == n - 1), tile_position=(0, HALF * c)) for c in range(2)]
                    return last

                def gate_up(e, it, j):
                    unit = UNIT["exp", l, 3 * j]

                    def body(w):
                        pe.wait_ge(drained[3], at(3, e) + 1)
                        pe.wait_ge(drained[4], at(4, e) + 1)
                        for c in range(2):
                            await_slot(it, unit + c)
                            await_bank_free(c, e)
                        ends = pair(w, [bank_e(0), bank_e(1)], lambda k: xgT[j][:, k, :],
                                    lambda c, k: slot(unit + c)[:, k, :], KD)
                        for c in range(2):
                            ends[c].then_inc(filled[c], 1)
                    by_width(pe, words, it, j, body)

                def turn_hidden(e, j):
                    pe.wait_ge(drained[1], at(1, e) + 1)
                    await_bank_free(2, e)
                    for c in range(KE):
                        last = pe.transpose(ps[:, 2, P * c:P * c + P], hid[j][:, c:DE:KE], ident)
                    last.then_inc(filled[2], 1)

                def down(e, it, j):
                    unit = UNIT["exp", l, 3 * j] + 2
                    wdn = slot(unit).rearrange("p k n -> p (k n)").rearrange("p (c n) -> p c n", c=KE)

                    def body(w):
                        pe.wait_ge(drained[2], at(2, e) + 1)
                        await_slot(it, unit)
                        for n in range(2):
                            await_bank_free(5 + n, e)
                        ends = pair(w, [bank_e(5), bank_e(6)], lambda k: hidT[j][:, k, :],
                                    lambda c, k: wdn[:, k, 512 * c:512 * c + 512], KE)
                        for c in range(2):
                            ends[c].then_inc(filled[5 + c], 1)
                    by_width(pe, words, it, j, body)

                words = wide_words(pe, l)
                turn_tokens(0, 0, 0)
                gate_up(0, 0, 0)
                turn_tokens(1, 0, 1)
                with pe.Fori(0, HE - 1) as it:
                    turn_hidden(2 * it, 0)
                    gate_up(2 * it + 1, it, 1)
                    down(2 * it, it, 0)
                    turn_tokens(2 * it + 2, it + 1, 0)
                    turn_hidden(2 * it + 1, 1)
                    gate_up(2 * it + 2, it + 1, 0)
                    down(2 * it + 1, it, 1)
                    turn_tokens(2 * it + 3, it + 1, 1)
                turn_hidden(NE - 2, 0)
                gate_up(NE - 1, HE - 1, 1)
                down(NE - 2, HE - 1, 0)
                turn_hidden(NE - 1, 1)
                down(NE - 1, HE - 1, 1)
                with on_overflow(pe, l):
                    with pe.Fori(0, NE * (NBLK - 1)) as n:
                        pe.wait_ge(over_xg[l], 16 * n + 16)
                        for k in range(KD):
                            last = pe.transpose(ps[:, 3 + k // 4, P * (k % 4):P * (k % 4) + P], xg[0][:, k:D:KD], ident)
                        last.then_inc(over_pe[l], 1)
                        pe.wait_ge(over_act[l], 4 * n + 1)
                        pe.wait_ge(over_dve[l], 3 * n + 1)
                        pe.wait_ge(over_w[l], 48 * n + 48)
                        for c in range(2):
                            last = product(bank_e(c), lambda k: xgT[0][:, k, :], lambda k: ring[:, c, k, :])
                        last.then_inc(over_pe[l], 1)
                        pe.wait_ge(over_dve[l], 3 * n + 2)
                        for c in range(KE):
                            last = pe.transpose(ps[:, 2, P * c:P * c + P], hid[0][:, c:DE:KE], ident)
                        last.then_inc(over_pe[l], 1)
                        pe.wait_ge(over_act[l], 4 * n + 3)
                        w = ring[:, 2, :, :].rearrange("p k n -> p (k n)").rearrange("p (c n) -> p c n", c=KE)
                        for h in range(2):
                            last = product(bank_e(5 + h), lambda c: hidT[0][:, c, :], lambda c: w[:, c, 512 * h:512 * h + 512], n=KE)
                        last.then_inc(over_pe[l], 1)

        @block.scalar
        def _(act):
            act.dma_start(modb[:, :, :], a["b_ada"].rearrange("l (v p k) -> p (l v) k", v=NMOD, k=KD)).then_inc(ada_in, 16)
            for n, name in enumerate(("g_norm1", "g_norm2")):
                act.dma_start(gcol[:, n], a[name].rearrange("l (p k) -> p l k", k=KD)).then_inc(ada_in, 16)
            act.wait_ge(consts_in, 32)
            act.activation(csil[:, :], ca[:, :], ACT.Silu).then_inc(silu_ready, 1)
            act.wait_ge(x_in, 16)

            def root_mean_square(t, before):
                s = ssum[:, t:t + 1]
                act.activation(xs[:, t, :], x[:, t, :], ACT.Square, accum_out=s).then_inc(sq_summed, 1)
                act.wait_ge(sq_summed, before + 1)
                act.activation(s, s, ACT.Sqrt, scale=1.0 / D, bias=C["eps"]).then_inc(sq_ready, 1)

            def squares(l, which, tiles=range(TT)):
                for t in tiles:
                    if which == 2:
                        act.wait_ge(mixed, 2 * (TT * l + t + 1))
                    root_mean_square(t, TT * (2 * l + which - 1) + t)

            def modulate(l, which, tiles=range(TT)):
                act.wait_ge(mod_ready, UNITS_ADA * l + (NORM1_UNITS if which == 1 else UNITS_ADA))
                for t in tiles:
                    key = (l, f"xT{which}", t, 0)
                    await_filled(act, key)
                    for q in range(4):
                        last = act.activation(hT[:, q, P * t:P * t + P], bank4(key)[:, q, :], ACT.Identity,
                                              scale=modc[:, 2 * which - 1, q:q + 1], bias=modc[:, 2 * which - 2, q:q + 1])
                    drains(last, key)

            def ada_out(l, u, part):
                await_filled(act, (l, "ada", u))
                drains(act.activation(tmp[:, part, :], bank((l, "ada", u)), ACT.Copy, scale=1 / 32), (l, "ada", u))

            def combine(l):
                for j in range(2):
                    act.wait_ge(yrow_out[j], 16 * HE * (l + 1))
                yv = yexp_d[l].rearrange("(k t p) d -> t k p d", k=2, p=P)
                for t in range(TT):
                    for k in range(2):
                        act.dma_start(yrow[t][k], yv[t, k]).then_inc(yrow_in[t], 16)
                for t in range(TT):
                    act.wait_ge(yrow_in[t], 32 * (l + 1))
                    act.activation(yrow[t][0], yrow[t][0], ACT.Copy, scale=gates[:, 0, t:t + 1]).then_inc(half_ready, 1)
                    if t >= 2:
                        act.wait_ge(x_done, TT * l + t - 1)
                        root_mean_square(t - 2, TT * (2 * l + 2) + t - 2)
                for t in (TT - 2, TT - 1):
                    act.wait_ge(x_done, TT * l + t + 1)
                    root_mean_square(t, TT * (2 * l + 2) + t)

            for l in range(DEPTH):
                if l == 0:
                    squares(l, 1)
                if l == 0:
                    for u in range(NORM1_UNITS):
                        ada_out(0, u, u % 2)
                modulate(l, 1)
                for f in range(2):
                    key = (l, "conv_in", 2 * f)
                    await_filled(act, key)
                    drains(act.activation(tmp[:, f, :], bank(key), ACT.Sigmoid), key)
                act.wait_ge(rin_lam, l + 1)
                act.activation(neglam[:, 0:2], neglam[:, 0:2], ACT.Exp).then_inc(rexp_lam, 1)
                for gi_, g in enumerate(GROUPS):
                    def qk_out(t):
                        key = (l, "qkT", g, t)
                        await_filled(act, key)
                        drains(act.activation(qkT[g][:, :, P * t:P * t + P], bank4(key), ACT.Copy), key)
                    for t in range(2):
                        qk_out(t)
                    for t in range(TT):
                        key = (l, "v", g, t)
                        await_filled(act, key)
                        drains(act.activation(v[g][:, t, :], bank(key)[:, 0:GW], ACT.Copy), key)
                        if t < 2:
                            qk_out(t + 2)

                def expo(i):
                    g = TILES[i][0]
                    for c in range(2 if g == "A" else 1):
                        n = map_no[(i, c)]
                        act.wait_ge(max_ready, NMAP * l + n + 1)
                        dst = prob_of(NQK + n)
                        if g == "A":
                            await_prob(act, l, NQK + n)
                            key = (l, "score", i, c)
                            drains(act.activation(dst[:, :], bank(key), ACT.Exp, scale=DIFF ** -0.5,
                                                  bias=negm[:, n:n + 1], accum_out=lsum[:, n:n + 1]), key)
                        else:
                            act.activation(dst[:, :], dst[:, :], ACT.Exp, scale=HD ** -0.5, bias=negm[:, n:n + 1],
                                           accum_out=lsum[:, n:n + 1]).then_inc(exp_ready, 1)

                def prob_out(i):
                    key = (l, "probT", i)
                    await_filled(act, key)
                    if i >= 2:
                        if i % 2:
                            await_filled(act, (l, "o", i // 2 - 1))
                        else:
                            act.wait_ge(pv_done, NOUT * l + i // 2)
                    drains(act.activation(probT[i % 2][:, :, :], bank4(key), ACT.Copy), key)

                def o_out(j):
                    key = (l, "oT", j)
                    g, hp, t, _ = TILES[2 * j]
                    await_filled(act, key)
                    if j == 2 * NA0:
                        act.wait_ge(conv_done[1], l + 1)
                    drains(act.activation(yT[:, FIRST_F[g] + hp, P * t:P * t + P], bank(key)[:, 0:P], ACT.Copy), key)

                def pad(i):
                    g, hp, t, h = TILES[i]
                    parts = 2 if g == "A" else 1
                    if i % (NTILE // 3) == 0:
                        act.wait_ge(pad_zeroed, 2 * l + (2 if g == "B" else 1))
                        await_drained(act, (l, "qkT", g, TT - 1))
                    for c in range(parts):
                        if i % (NTILE // 3) >= 2:
                            await_filled(act, (l, "score", i - 2, c))
                        n = HD // parts
                        p0 = HD * h + n * c
                        act.activation(qpad[g][2 * h + c if g == "A" else h][p0:p0 + n, :],
                                       qkT[g][p0:p0 + n, hp, P * t:P * t + P], ACT.Copy).then_inc(pad_ready, 1)

                for i in range(2):
                    pad(i)
                for i in range(NSTEP):
                    if i < NTILE:
                        expo(i)
                    if i + 2 < NTILE:
                        pad(i + 2)
                    if 2 <= i < NTILE + 2:
                        prob_out(i - 2)
                    for j in leaves(i):
                        o_out(j)
                    n = ada_at(l, i)
                    if n is not None:
                        m, u = ADA_LATER[l][n]
                        if n >= 2:
                            await_filled(act, (ADA_LATER[l][n - 2][0], "mod", ADA_LATER[l][n - 2][1]))
                        ada_out(m, u, n % 2)
                    if i == ROOT_STEP:
                        act.wait_ge(oss_ready, l + 1)
                        act.activation(oss[:, :], oss[:, :], ACT.Sqrt, scale=1.0 / HD, bias=C["eps"]).then_inc(oss_root, 1)
                        for f in range(2):
                            key = (l, "var", f)
                            await_filled(act, key)
                            act.activation(tmp[:, f, :], bank(key), ACT.Ln, bias=C["eps"]).then_inc(log_ready, 1)
                        for f in range(2):
                            key = (l, "var", f)
                            act.wait_ge(log_ready, 2 * l + f + 1)
                            drains(act.activation(tmp[:, f, :], tmp[:, f, :], ACT.Exp, scale=-0.5), key)
                    if i == NTILE + 2:
                        for f in range(2):
                            act.wait_ge(norm_ready, 2 * l + f + 1)
                            act.activation(yT[:, FIRST_F["C"] + f, :], z[:, f, HALO:HALO + S], ACT.Silu,
                                           scale=convp[:, 1, f:f + 1], bias=convp[:, 2, f:f + 1]).then_inc(conv_ready, 1)
                for t in range(TT + 1):
                    if t:
                        act.wait_ge(xs_ready, TT * (2 * l + 1) + t)
                        act.dma_start(xn2_d[l].rearrange("(t p) d -> t p d", p=P)[t - 1], xs[:, t - 1, :]).then_inc(xn_out, 16)
                        modulate(l, 2, [t - 1])
                    if t < TT:
                        squares(l, 2, [t])
                for n, (m, u) in enumerate(ADA_NEXT[l][:2]):
                    ada_out(m, u, n)
                for n in range(2):
                    act.wait_ge(rin_ready, 2 * l + n + 1)
                    r = rt[:, 0:16] if n == 0 else rt[:, 16:20]
                    act.activation(r, r, ACT.Exp).then_inc(rexp_ready, 1)
                for n, (m, u) in enumerate(ADA_NEXT[l][2:]):
                    await_filled(act, (m, "mod", u - 2))
                    ada_out(m, u, n)

                def at(b, e):
                    return e + expert_bank(l, b)

                def expert_tokens(e, j):
                    act.wait_ge(filled[3], at(3, e) + 1)
                    if not isinstance(e, int) or e >= 2:
                        act.wait_ge(filled[1], at(1, e) - 1)
                    for q in range(4):
                        last = act.activation(xgT[j][:, q, :], ps[:, 3, P * q:P * q + P], ACT.Identity,
                                              scale=modc[:, 3, q:q + 1], bias=modc[:, 2, q:q + 1])
                    last.then_inc(drained[3], 1)

                def expert_silu(e, j):
                    act.wait_ge(filled[0], at(0, e) + 1)
                    if not isinstance(e, int) or e >= 2:
                        act.wait_ge(drained[1], at(1, e) - 1)
                    act.activation(sil[j], ps[:, 0, :], ACT.Silu).then_inc(drained[0], 1)

                def expert_hidden(e, j):
                    act.wait_ge(filled[2], at(2, e) + 1)
                    if not isinstance(e, int) or e >= 2:
                        act.wait_ge(filled[6], at(6, e) - 1)
                    act.activation(hidT[j].rearrange("p c s -> p (c s)"), ps[:, 2, :], ACT.Copy).then_inc(drained[2], 1)

                def expert_rows(e, it, j):
                    def body(w):
                        act.wait_ge(filled[5], at(5, e) + 1)
                        if not isinstance(it, int) or it >= 1 or l:
                            act.wait_ge(yrow_out[j], 16 * it + 16 * l * HE)
                        act.activation(yexp[j][0:w, 0:512], ps[0:w, 5, :], ACT.Copy).then_inc(drained[5], 1)
                    by_width(act, words, it, j, body)

                words = wide_words(act, l)
                expert_tokens(0, 0)
                expert_silu(0, 0)
                expert_tokens(1, 1)
                expert_hidden(0, 0)
                expert_silu(1, 1)
                expert_rows(0, 0, 0)
                expert_tokens(2, 0)
                expert_hidden(1, 1)
                expert_silu(2, 0)
                expert_rows(1, 0, 1)
                expert_tokens(3, 1)
                with act.Fori(1, HE - 1) as it:
                    expert_hidden(2 * it, 0)
                    expert_silu(2 * it + 1, 1)
                    expert_rows(2 * it, it, 0)
                    expert_tokens(2 * it + 2, 0)
                    expert_hidden(2 * it + 1, 1)
                    expert_silu(2 * it + 2, 0)
                    expert_rows(2 * it + 1, it, 1)
                    expert_tokens(2 * it + 3, 1)
                expert_hidden(NE - 2, 0)
                expert_silu(NE - 1, 1)
                expert_rows(NE - 2, HE - 1, 0)
                expert_hidden(NE - 1, 1)
                expert_rows(NE - 1, HE - 1, 1)
                with on_overflow(act, l):
                    with act.Fori(0, NE * (NBLK - 1)) as n:
                        act.wait_ge(over_pe[l], 4 * n + 1)
                        for q in range(4):
                            last = act.activation(xgT[0][:, q, :], ps[:, 3, P * q:P * q + P], ACT.Identity,
                                                  scale=modc[:, 3, q:q + 1], bias=modc[:, 2, q:q + 1])
                        last.then_inc(over_act[l], 1)
                        act.wait_ge(over_pe[l], 4 * n + 2)
                        act.activation(sil[0], ps[:, 0, :], ACT.Silu).then_inc(over_act[l], 1)
                        act.wait_ge(over_pe[l], 4 * n + 3)
                        act.activation(hidT[0].rearrange("p c s -> p (c s)"), ps[:, 2, :], ACT.Copy).then_inc(over_act[l], 1)
                        act.wait_ge(over_pe[l], 4 * n + 4)
                        act.activation(yexp[0][:, 0:512], ps[:, 5, :], ACT.Copy).then_inc(over_act[l], 1)
                with on_overflow(act, l):
                    act.wait_ge(over_out[l], 16 * NE * (NBLK - 1))
                combine(l)

        @block.vector
        def _(dve):
            chain = [0]

            def link(ins):
                chain[0] += 1
                ins.then_inc(dve_chain, 1)
                dve.wait_ge(dve_chain, chain[0])

            dve.wait_ge(consts_in, 32)
            dve.wait_ge(silu_ready, 1)
            dve.tensor_tensor(ca_rep[:, :, :], view(cst, C_AT["ones"], [[NCONST, P], [0, KD], [1, 32]]),
                              view(csil, 0, [[KD, P], [1, KD], [0, 32]]), ALU.mult).then_inc(ca_ready, 1)

            def normalise(l, which, tiles=range(TT)):
                for t in tiles:
                    dve.wait_ge(sq_ready, TT * (2 * l + which - 1) + t + 1)
                    r = rstd[:, t:t + 1]
                    link(dve.reciprocal(r, ssum[:, t:t + 1]))
                    if l == DEPTH:
                        if t == 0:
                            dve.wait_ge(gfin_in, 16)
                        dve.scalar_tensor_tensor(x[:, t, :], x[:, t, :], r, gate[:, 0, :], ALU.mult, ALU.mult).then_inc(fin_ready, 1)
                        continue
                    dve.tensor_scalar(xs[:, t, :], x[:, t, :], r, None, ALU.mult).then_inc(xs_ready, 1)

            def modulate(l, which, tiles=range(TT)):
                for t in tiles:
                    key = (l, f"xT{which}", t, 1)
                    await_filled(dve, key)
                    for q in range(4):
                        k = 4 + q
                        last = dve.tensor_scalar(hT[:, k, P * t:P * t + P], bank4(key)[:, q, :], modc[:, 2 * which - 1, k:k + 1],
                                                 modc[:, 2 * which - 2, k:k + 1], ALU.mult, ALU.add)
                    drains(last, key)

            def mod_out(l, u):
                key, m = (l, "mod", u), u // 2
                await_filled(dve, key)
                if m % 3 == 2:
                    gv = gate[:, m // 3, 512 * (u % 2):512 * (u % 2) + 512]
                    dve.tensor_tensor(gv, bank(key), gv, ALU.add).then_inc(dve_chain, 1)
                else:
                    p = slice(HALF * (u % 2), HALF * (u % 2) + HALF)
                    c = modc[p, 2 * (m // 3) + m % 3, :]
                    dve.tensor_tensor(c, bank(key)[p, 0:KD], modb[p, NMOD * l + m, :], ALU.add).then_inc(dve_chain, 1)
                chain[0] += 1
                dve.wait_ge(dve_chain, chain[0])
                if m % 3 == 1:
                    link(dve.scalar_tensor_tensor(c, c, 1.0, gcol[p, m // 3, l, :], ALU.add, ALU.mult))
                dve.sem_inc(mod_ready, 1)
                dve.sem_inc(drained[bank_of[key][0]], 1)

            dve.wait_ge(x_in, 16)
            dve.wait_ge(ada_in, 48)
            for l in range(DEPTH):
                if l == 0:
                    normalise(l, 1)
                    for u in range(NORM1_UNITS):
                        mod_out(0, u)
                dve.wait_ge(mod_ready, UNITS_ADA * l + NORM1_UNITS)
                modulate(l, 1)
                dve.wait_ge(params_in, 16 * N_PARAMS * (l + 1))
                lv = lamrow.rearrange("p (a b c) -> p a b c", a=2, b=2)
                link(dve.tensor_tensor(lam.rearrange("p (a c) -> p a c", a=2), lv[:, :, 0, :], lv[:, :, 1, :], ALU.mult))
                dve.tensor_reduce(neglam[:, 0:2], lam.rearrange("p (a c) -> p a c", a=2), AX_X, ALU.add).then_inc(rin_lam, 1)
                dve.wait_ge(rexp_lam, l + 1)
                link(dve.tensor_tensor(neglam[:, 2:3], neglam[:, 1:2], neglam[:, 0:1], ALU.subtract))
                link(dve.tensor_scalar(neglam[:, 2:3], neglam[:, 2:3], -SUBLN_INIT[l], None, ALU.add))
                link(dve.tensor_scalar(subg[:, :], subg[:, :], 1.0 - SUBLN_INIT[l], None, ALU.mult))
                dve.wait_ge(halo_ready, 2)
                for f in range(2):
                    key = (l, "conv_in", 2 * f + 1)
                    await_drained(dve, (l, "conv_in", 2 * f))
                    await_filled(dve, key)
                    drains(dve.tensor_tensor(z[:, f, HALO:HALO + S], bank(key), tmp[:, f, :], ALU.mult), key)
                for gi_, g in enumerate(GROUPS):
                    for t in range(TT):
                        key, n = (l, "qk", g, t), gi_ * TT + t
                        await_filled(dve, key)
                        await_prob(dve, l, n)
                        if n:
                            dve.wait_ge(rot_ready, NQK * l + n)
                        else:
                            await_drained(dve, (l, "conv_in", 3))
                        dst = prob_of(n)
                        if g == "B":
                            drains(dve.tensor_copy(dst[:, :], bank(key)), key)
                            dve.wait_ge(drained[bank_of[key][0]], bank_of[key][1] + 1)
                            dve.sem_inc(rot_ready, 1)
                            continue
                        w = HD if g == "D" else DIFF
                        hw, ng = w // 2, 512 // w
                        cos = view(cst, C_AT["cos" + g] + w * t, [[NCONST, P], [0, ng], [1, w]])
                        src = bank(key).rearrange("p (g w) -> p g w", w=w)
                        tc = tmp[:, 0, :].rearrange("p (g w) -> p g w", w=w)
                        tsn = tmp[:, 1, :].rearrange("p (g w) -> p g w", w=w)
                        dve.tensor_tensor(tc, src, cos, ALU.mult)
                        for half in range(2):
                            sin = view(cst, C_AT["sin" + g] + w * t + hw * half, [[NCONST, P], [0, ng], [1, hw]])
                            last = dve.tensor_tensor(tsn[:, :, hw * half:hw * half + hw], src[:, :, hw * (1 - half):hw * (2 - half)],
                                                     sin, ALU.mult)
                        drains(last, key)
                        await_drained(dve, key)
                        dve.tensor_tensor(dst[:, :], tmp[:, 0, :], tmp[:, 1, :], ALU.add).then_inc(rot_ready, 1)

                def maxima(i):
                    g, hp, t, h = TILES[i]
                    for c in range(2 if g == "A" else 1):
                        n = map_no[(i, c)]
                        key = (l, "score", i, c)
                        await_filled(dve, key)
                        if g == "A":
                            link(dve.tensor_reduce(mx[:, n:n + 1], bank(key), AX_X, ALU.max))
                            dve.tensor_scalar(negm[:, n:n + 1], mx[:, n:n + 1], -DIFF ** -0.5, None, ALU.mult).then_inc(max_ready, 1)
                            continue
                        if i == 0:
                            dve.wait_ge(table_in, 16 * N_TABLES * (l + 1))
                        if g == "B":
                            dve.wait_ge(bias_ready, 4 * l + 2 * (hp + 1))
                        if g == "D":
                            table = dil[:, P * (TT - 1 - t):P * (TT - 1 - t) + S]
                        else:
                            first = (RPB_H - 1) * GRID_W * h + (GRID_H - 2 - 2 * t) * GRID_W
                            table = bias_t[hp][:, first:first + S]
                        await_prob(dve, l, NQK + n)
                        drains(dve.tensor_tensor_reduce(prob_of(NQK + n)[:, :], bank(key), table, 1.0, -3.0e38, ALU.add, ALU.max,
                                                        mx[:, n:n + 1]), key)
                        await_drained(dve, key)
                        dve.tensor_scalar(negm[:, n:n + 1], mx[:, n:n + 1], -HD ** -0.5, None, ALU.mult).then_inc(max_ready, 1)

                def mix(i):
                    n = map_no[(i, 0)]
                    for c in range(2):
                        await_drained(dve, (l, "score", i, c))
                    link(dve.reciprocal(rinv[:, n:n + 2], lsum[:, n:n + 2]))
                    link(dve.tensor_tensor(coef[:, 0:1], lsum[:, n:n + 1], rinv[:, n + 1:n + 2], ALU.mult))
                    link(dve.tensor_tensor(coef[:, 1:2], coef[:, 0:1], neglam[:, 2:3], ALU.mult))
                    p0, p1 = prob_of(NQK + n), prob_of(NQK + n + 1)
                    dve.scalar_tensor_tensor(p0[:, :], p1[:, :], coef[:, 1:2], p0[:, :], ALU.mult, ALU.add).then_inc(mix_ready, 1)

                def heads_out(j):
                    g = TILES[2 * j][0]
                    key = (l, "o", j)
                    n = map_no[(2 * j, 0)]
                    step = 2 if g == "A" else 1
                    rv = view(rinv, n, [[NMAP, P], [step, 2], [0, HD]])
                    o = bank(key)[:, 0:P].rearrange("p (h e) -> p h e", h=2)
                    y = (yA[:, j - NA0, :] if g == "A" else ytok[:, :]).rearrange("p (h e) -> p h e", h=2)
                    if g != "A":
                        dve.wait_ge(exp_ready, 2 * NTILE // 3 * l + (2 * j if g == "D" else 2 * j - NTILE // 3) + 2)
                        link(dve.reciprocal(rinv[:, n:n + 2], lsum[:, n:n + 2]))
                    await_filled(dve, key)
                    if g != "A" and j:
                        await_filled(dve, (l, "oT", j - 1 if j != 2 * NA0 else NA0 - 1))
                    drains(dve.tensor_tensor(y, o, rv, ALU.mult), key)

                def subln(part):
                    y = yA.rearrange("p j (h e) -> p (j h) e", h=2)
                    if part == 0:
                        sq = yT[:, 0:2, :].rearrange("p a (j e) -> p (a j) e", e=HD)
                        await_drained(dve, (l, "o", 2 * NA0 - 1))
                        link(dve.tensor_tensor(sq, y, y, ALU.mult))
                        dve.tensor_reduce(oss[:, :], sq, AX_X, ALU.add).then_inc(oss_ready, 1)
                        return
                    dve.wait_ge(oss_root, l + 1)
                    link(dve.reciprocal(oss[:, :], oss[:, :]))
                    link(dve.tensor_tensor(y, y, view(oss, 0, [[2 * NA0, P], [1, 2 * NA0], [0, HD]]), ALU.mult))
                    dve.tensor_tensor(y, y, view(subg, 0, [[HD, P], [0, 2 * NA0], [1, HD]]), ALU.mult).then_inc(yA_ready, 1)

                def tap(f, k):
                    acc = yT[:, FIRST_F["C"] + f, :]
                    w = convw[:, f, k:k + 1]
                    if k == 0:
                        link(dve.tensor_scalar(acc, z[:, f, 0:S], w, convp[:, 0, f:f + 1], ALU.mult, ALU.add))
                        return
                    ins = dve.scalar_tensor_tensor(acc, z[:, f, k:k + S], w, acc, ALU.mult, ALU.add)
                    if k == (TAPS, DVE_TAPS)[f] - 1:
                        ins.then_inc((conv_done[0], conv_part)[f], 1)
                    else:
                        link(ins)

                def centre(f):
                    key = (l, "mean", f)
                    zc = z[:, f, HALO:HALO + S]
                    if f == 0:
                        m, u = ADA_LATER[l][-1]
                        await_filled(dve, (m, "mod", u))
                    await_filled(dve, key)
                    drains(dve.tensor_tensor(zc, yT[:, FIRST_F["C"] + f, :], bank(key), ALU.subtract), key)
                    await_drained(dve, key)
                    dve.tensor_tensor(tmp[:, f, :], zc, zc, ALU.mult).then_inc(stat_ready, 1)

                def deviate(f):
                    zc = z[:, f, HALO:HALO + S]
                    await_drained(dve, (l, "var", f))
                    dve.tensor_tensor(zc, zc, tmp[:, f, :], ALU.mult).then_inc(norm_ready, 1)

                await_filled(dve, (l, "v", "B", TT - 1))
                dve.memset(yT[:, 0:2, :], 0.0).then_inc(pad_zeroed, 1)
                for i in range(NTILE + 4):
                    if i < NTILE:
                        maxima(i)
                    if i == NTILE // 3:
                        dve.memset(masks[:, 0, 0:2 * P], 0.0).then_inc(pad_zeroed, 1)
                    if 1 <= i <= NTILE and TILES[i - 1][0] == "A":
                        mix(i - 1)
                    for f in range(2):
                        if 0 <= i - 2 < (TAPS, DVE_TAPS)[f]:
                            tap(f, i - 2)
                    if i >= 5 and i % 2 == 1:
                        heads_out((i - 5) // 2)
                    if ada_at(l, i - 1) is not None:
                        mod_out(*ADA_LATER[l][ada_at(l, i - 1)])
                    if i == SUBLN_STEP:
                        subln(0)
                    if i == ROOT_STEP + 1:
                        subln(1)
                    if i == SUBLN_STEP:
                        for f in range(2):
                            centre(f)
                    if 2 <= i - ROOT_STEP < 4:
                        deviate(i - ROOT_STEP - 2)

                for t in range(TT + 1):
                    if t < TT:
                        for n in range(2):
                            key = (l, "out", t, n)
                            await_filled(dve, key)
                            if t:
                                dve.wait_ge(mixed, 2 * (TT * l + t - 1) + n + 1)
                            drains(dve.tensor_tensor(tmp[:, n, :], bank(key), gate[:, 0, 512 * n:512 * n + 512], ALU.mult), key)
                    if t:
                        modulate(l, 2, [t - 1])
                    if t < TT:
                        normalise(l, 2, [t])
                route(dve, link, mod_out, l)
                experts_dve(dve, l)
                for t in range(TT):
                    dve.wait_ge(yrow_in[t], 32 * (l + 1))
                    dve.wait_ge(half_ready, TT * l + t + 1)
                    y0, y1 = yrow[t]
                    link(dve.scalar_tensor_tensor(y0, y1, gates[:, 1, t:t + 1], y0, ALU.mult, ALU.add))
                    dve.tensor_tensor(y0, y0, gate[:, 1, :], ALU.mult).then_inc(comb_ready, 1)
                    if t >= TT // 2:
                        dve.wait_ge(comb_ready, TT * l + t + 1)
                        dve.wait_ge(x_done, TT * l + t)
                        dve.tensor_tensor(x[:, t, :], x[:, t, :], y0, ALU.add).then_inc(x_done, 1)
                    if t >= 2:
                        normalise(l + 1, 1, [t - 2])
                normalise(l + 1, 1, [TT - 2, TT - 1])


_INS = ["x", "c", "na_rpb", "w_ada", "b_ada", "g_norm1", "g_norm2", "w_in", "diff_lambda", "diff_subln", "conv_dw", "conv_b",
        "conv_norm_g", "conv_norm_b", "w_out", "w_router_group", "w_router_expert", "w_exp_gate", "w_exp_up",
        "w_exp_down", "g_final"]


def shape_constants():
    import numpy as np
    out = {}
    out["ident"] = np.eye(P)
    out["before"] = np.triu(np.ones((P, P)), 1)
    out["groupmean"] = np.kron(np.eye(2), np.ones((HD, HD)) / HD)
    out["ones"] = np.ones((P, P))
    out["iota"] = np.tile(np.arange(P), (P, 1))
    out["ids"] = np.arange(2 * TT)[None] * P + np.arange(P)[:, None] + 1
    out["bit"] = np.tile(2.0 ** (np.arange(NE) // 2), (P, 1))
    out["first"] = np.tile(np.arange(NG, 0, -1), (P, 1))
    for g, w in (("A", DIFF), ("D", HD)):
        inv = np.float32(10000.0) ** (-np.arange(0, w, 2, dtype=np.float32) / np.float32(w))
        ang = (np.arange(S, dtype=np.float32)[:, None] * inv.astype(np.float32)[None, :]).astype(np.float64)
        cos, sin = np.cos(ang), np.sin(ang)
        for name, tab in (("cos", np.concatenate([cos, cos], 1)), ("sin", np.concatenate([-sin, sin], 1))):
            out[name + g] = tab.reshape(TT, P, w).transpose(1, 0, 2).reshape(P, TT * w)
    col = np.arange(GRID_W)
    start = np.clip(col - NA_W // 2, 0, GRID_W - NA_W)
    ok = (col[None] >= start[:, None]) & (col[None] < start[:, None] + NA_W)
    out["colmask"] = np.tile(np.where(ok, 0.0, NEG), (2, 1))
    out["eps"] = np.full((P, 1), EPS)
    table = np.concatenate([out[k] for k in CONSTS], 1).astype(np.float32)
    rel = np.arange(2 * S - P)[None] - (S - P) - np.arange(P)[:, None]
    count = sum(((rel % dil == 0) & (np.abs(rel) <= win // (2 * dil) * dil)).astype(int)
                for win, dil in ((128, 1), (512, 4), (2048, 16)))
    dil = np.where(count > 0, HD ** 0.5 * np.log(np.maximum(count, 1)), NEG).astype(np.float32)
    return table, dil


def kernel(**inputs):
    import numpy as np
    import concourse.bacc as bacc
    from concourse.bass_utils import run_bass_kernel_spmd

    nc = bacc.Bacc("TRN2", target_bir_lowering=False, num_devices=1)
    arrays = {n: np.ascontiguousarray(inputs[n]) for n in _INS}
    arrays["conv_dw"] = np.ascontiguousarray(np.transpose(arrays["conv_dw"], (0, 2, 1)))
    col = np.arange(GRID_W)
    dc = np.clip(col[None] - col[:, None], -(RPB_W // 2), RPB_W // 2) + RPB_W // 2
    arrays["rpb"] = np.ascontiguousarray(np.moveaxis(arrays.pop("na_rpb")[..., dc], 2, 3)).reshape(DEPTH, NH, GRID_W, RPB_H * GRID_W)
    arrays["consts"], arrays["dilation"] = shape_constants()
    aps = {n: nc.dram_tensor(f"in_{n}", v.shape, mybir.dt.from_np(v.dtype), kind="ExternalInput").ap()
           for n, v in arrays.items()}
    aps["out"] = nc.dram_tensor("out_0", (1, S, D), F32, kind="ExternalOutput").ap()
    program(nc, aps)
    r = run_bass_kernel_spmd(nc, [{f"in_{n}": v for n, v in arrays.items()}], core_ids=[0])
    return r.results[0]["out_0"]
```
